# Optimizing a Trainium2 kernel written in Bass

```python
import jax
import jax.numpy as jnp
from jax import lax
import numpy as np

D_MODEL = 1024
BATCH = 1
SEQ = 256
DEPTH = 4
DEC_BATCH = 8
DEC_SEQ = 8
PAST_LEN = 2048
PAGE_SIZE = 128

F32 = jnp.float32
N_MIXERS = 3
N_A = (DEPTH + 2) // N_MIXERS
N_B = (DEPTH + 1) // N_MIXERS
N_C = DEPTH // N_MIXERS
EXPAND = 2
BRANCH = EXPAND * D_MODEL
CONV_W = 4
EPS = 1e-6

LRU_WIDTH = BRANCH
LRU_BLOCKS = 8
LRU_BLOCK = LRU_WIDTH // LRU_BLOCKS
LRU_C = 8.0

SSD_HEAD_DIM = 64
SSD_HEADS = BRANCH // SSD_HEAD_DIM
SSD_STATE = 128
SSD_GROUPS = 8
SSD_CONV_DIM = BRANCH + 2 * SSD_GROUPS * SSD_STATE
SSD_CHUNK = 128

HGRN_KEY_DIM = 128
HGRN_HEADS = BRANCH // HGRN_KEY_DIM
HGRN_VAL_DIM = BRANCH // HGRN_HEADS
HGRN_CHUNK = 16

N_MEM = 256
X_HEADS = 4
X_HEAD_DIM = D_MODEL // X_HEADS

kernel_name = 'hybrid_rglru_ssd_hgrn2_memxattn_step'

def rms_norm(x, g):
    xf = x.astype(F32)
    y = xf * lax.rsqrt(jnp.mean(xf * xf, axis=-1, keepdims=True) + EPS)
    return (y * g.astype(F32)).astype(x.dtype)

def causal_conv(u, state, w, b):
    L = u.shape[1]
    uu = jnp.concatenate([state.astype(u.dtype), u], axis=1)
    y = b + w[0] * uu[:, 0:L]
    for k in range(1, CONV_W):
        y = y + w[k] * uu[:, k:k + L]
    return y, uu[:, L:]

def linear_scan(a, b):
    def combine(left, right):
        a_l, b_l = left
        a_r, b_r = right
        return a_l * a_r, a_r * b_l + b_r
    _, h = lax.associative_scan(combine, (a, b), axis=1)
    return h

def pad_seq(t, pad):
    if pad == 0:
        return t
    widths = [(0, 0)] * t.ndim
    widths[1] = (0, pad)
    return jnp.pad(t, widths)

def rglru_mixer(x, conv_state, h0, w_in, conv_w, conv_b, w_a, b_a, w_x, b_x, lam, w_out):
    bsz, L, _ = x.shape
    u, gate = jnp.split(x @ w_in, 2, axis=-1)
    u, new_conv = causal_conv(u, conv_state, conv_w, conv_b)
    ub = u.reshape(bsz, L, LRU_BLOCKS, LRU_BLOCK)
    r = jax.nn.sigmoid((jnp.einsum('blhi,hij->blhj', ub, w_a).reshape(bsz, L, LRU_WIDTH) + b_a).astype(F32))
    i = jax.nn.sigmoid((jnp.einsum('blhi,hij->blhj', ub, w_x).reshape(bsz, L, LRU_WIDTH) + b_x).astype(F32))
    log_a = -LRU_C * r * jax.nn.softplus(-lam.astype(F32))
    a = jnp.exp(log_a)
    b = jnp.sqrt(-jnp.expm1(2.0 * log_a)) * (i * u.astype(F32))
    b = b.at[:, 0].add(a[:, 0] * h0.astype(F32))
    h = linear_scan(a, b)
    y = (h.astype(x.dtype) * jax.nn.silu(gate)) @ w_out
    return y, new_conv, h[:, -1].astype(x.dtype)

def ssd_chunked(xs, dt, a, bm, cm, s0):
    bsz, L, H, P = xs.shape
    G, N = SSD_GROUPS, SSD_STATE
    J = H // G
    Q = min(SSD_CHUNK, L)
    pad = (-L) % Q
    xs, dt, bm, cm = (pad_seq(t, pad) for t in (xs, dt, bm, cm))
    nc = (L + pad) // Q
    x = xs.reshape(bsz, nc, Q, G, J, P)
    dt = dt.reshape(bsz, nc, Q, G, J)
    bc = bm.reshape(bsz, nc, Q, G, N)
    cc = cm.reshape(bsz, nc, Q, G, N)
    acs = jnp.cumsum(dt * a.reshape(G, J), axis=2)
    xdt = x * dt[..., None]
    causal = jnp.tril(jnp.ones((Q, Q), dtype=bool))[:, :, None, None]
    seg = acs[:, :, :, None] - acs[:, :, None, :]
    decay = jnp.exp(jnp.where(causal, seg, -jnp.inf))
    cb = jnp.einsum('bclgn,bcsgn->bclsg', cc, bc)
    y_diag = jnp.einsum('bclsg,bclsgj,bcsgjp->bclgjp', cb, decay, xdt)
    decay_states = jnp.exp(acs[:, :, -1:] - acs)
    states = jnp.einsum('bclgn,bclgj,bclgjp->bcgjpn', bc, decay_states, xdt)
    chunk_decay = jnp.exp(acs[:, :, -1])

    def step(s, inp):
        st, dec = inp
        return s * dec[..., None, None] + st, s

    s_final, starts = lax.scan(step, s0.reshape(bsz, G, J, P, N),
                               (jnp.moveaxis(states, 1, 0), jnp.moveaxis(chunk_decay, 1, 0)))
    starts = jnp.moveaxis(starts, 0, 1)
    y_off = jnp.einsum('bclgn,bcgjpn,bclgj->bclgjp', cc, starts, jnp.exp(acs))
    y = (y_diag + y_off).reshape(bsz, nc * Q, H, P)[:, :L]
    return y, s_final.reshape(bsz, H, P, N)

def ssd_mixer(x, conv_state, s0, w_in, conv_w, conv_b, dt_bias, a_log, d_skip, norm_g, w_out):
    bsz, L, _ = x.shape
    proj = x @ w_in
    z = proj[..., :BRANCH]
    xbc = proj[..., BRANCH:BRANCH + SSD_CONV_DIM]
    dt_raw = proj[..., BRANCH + SSD_CONV_DIM:]
    xbc, new_conv = causal_conv(xbc, conv_state, conv_w, conv_b)
    xbc = jax.nn.silu(xbc).astype(F32)
    gn = SSD_GROUPS * SSD_STATE
    xs = xbc[..., :BRANCH].reshape(bsz, L, SSD_HEADS, SSD_HEAD_DIM)
    bm = xbc[..., BRANCH:BRANCH + gn].reshape(bsz, L, SSD_GROUPS, SSD_STATE)
    cm = xbc[..., BRANCH + gn:].reshape(bsz, L, SSD_GROUPS, SSD_STATE)
    dt = jax.nn.softplus(dt_raw.astype(F32) + dt_bias.astype(F32))
    a = -jnp.exp(a_log.astype(F32))
    y, s_new = ssd_chunked(xs, dt, a, bm, cm, s0.astype(F32))
    y = y + d_skip.astype(F32)[:, None] * xs
    y = y.reshape(bsz, L, BRANCH) * jax.nn.silu(z.astype(F32))
    yg = y.reshape(bsz, L, SSD_GROUPS, BRANCH // SSD_GROUPS)
    yg = yg * lax.rsqrt(jnp.mean(yg * yg, axis=-1, keepdims=True) + EPS)
    y = yg.reshape(bsz, L, BRANCH) * norm_g.astype(F32)
    return y.astype(x.dtype) @ w_out, new_conv, s_new.astype(x.dtype)

def gla_chunked(q, k, v, g, s0):
    bsz, L, H, _ = q.shape
    DV = v.shape[-1]
    Q = min(HGRN_CHUNK, L)
    pad = (-L) % Q
    nc = (L + pad) // Q

    def chunks(t):
        t = pad_seq(t, pad)
        return jnp.moveaxis(t.reshape(bsz, nc, Q, H, t.shape[-1]), 1, 0)

    causal = jnp.tril(jnp.ones((Q, Q), dtype=bool))

    def step(S, inp):
        qc, kc, vc, gc = inp
        G = jnp.cumsum(gc, axis=1)
        qg = qc * jnp.exp(G)
        att = jnp.einsum('blhd,bshd->bhls', qg, kc * jnp.exp(-G))
        att = jnp.where(causal, att, 0.0)
        o = jnp.einsum('bhls,bshv->blhv', att, vc) + jnp.einsum('blhd,bhdv->blhv', qg, S)
        g_last = G[:, -1]
        S = S * jnp.exp(g_last)[..., None] + jnp.einsum('bshd,bshv->bhdv', kc * jnp.exp(g_last[:, None] - G), vc)
        return S, o

    s_final, o = lax.scan(step, s0, (chunks(q), chunks(k), chunks(v), chunks(g)))
    o = jnp.moveaxis(o, 0, 1).reshape(bsz, nc * Q, H, DV)[:, :L]
    return o, s_final

def hgrn2_mixer(x, s0, lb, w_in, norm_g, w_out):
    bsz, L, _ = x.shape
    q, f, v, gate = jnp.split(x @ w_in, 4, axis=-1)
    shp = (bsz, L, HGRN_HEADS, HGRN_KEY_DIM)
    lb = lb.astype(F32)
    f = f.astype(F32)
    forget = lb + (1.0 - lb) * jax.nn.sigmoid(f)
    log_f = jnp.log(forget).reshape(shp)
    k = ((1.0 - lb) * jax.nn.sigmoid(-f)).reshape(shp)
    q = jax.nn.silu(q.astype(F32)).reshape(shp)
    v = v.astype(F32).reshape(bsz, L, HGRN_HEADS, HGRN_VAL_DIM)
    o, s_new = gla_chunked(q, k, v, log_f, s0.astype(F32))
    o = o * lax.rsqrt(jnp.mean(o * o, axis=-1, keepdims=True) + EPS)
    o = o.reshape(bsz, L, BRANCH) * norm_g.astype(F32) * jax.nn.silu(gate.astype(F32))
    return o.astype(x.dtype) @ w_out, s_new.astype(x.dtype)

def memory_kv(mem, g, w_k, w_v):
    m = rms_norm(mem, g)
    shp = mem.shape[:2] + (X_HEADS, X_HEAD_DIM)
    return (m @ w_k).reshape(shp), (m @ w_v).reshape(shp)

def memory_cross_attn(x, mem_k, mem_v, w_q, w_o):
    bsz, L, _ = x.shape
    q = (x @ w_q).reshape(bsz, L, X_HEADS, X_HEAD_DIM)
    s = jnp.einsum('blhd,bmhd->bhlm', q, mem_k.astype(q.dtype)).astype(F32) * (X_HEAD_DIM ** -0.5)
    p = jax.nn.softmax(s, axis=-1).astype(x.dtype)
    o = jnp.einsum('bhlm,bmhd->blhd', p, mem_v.astype(x.dtype)).reshape(bsz, L, D_MODEL)
    return o @ w_o

def run_trunk(x, mem_k, mem_v, rg_conv0, rg_h0, ssd_conv0, ssd_s0, hg_s0, P):
    cum = jnp.cumsum(jax.nn.softmax(P['hg_lower_bounds'].astype(F32), axis=0), axis=0)
    lower_bounds = cum - cum[0]
    rg_conv, rg_h, ssd_conv, ssd_s, hg_s = [], [], [], [], []
    for layer in range(DEPTH):
        kind, idx = layer % N_MIXERS, layer // N_MIXERS
        g = P['norm_g'][layer]
        h = rms_norm(x, g[0])
        if kind == 0:
            y, c_new, h_new = rglru_mixer(h, rg_conv0[idx], rg_h0[idx], P['rg_w_in'][idx], P['rg_conv_w'][idx],
                                          P['rg_conv_b'][idx], P['rg_w_a'][idx], P['rg_b_a'][idx], P['rg_w_x'][idx],
                                          P['rg_b_x'][idx], P['rg_lambda'][idx], P['rg_w_out'][idx])
            rg_conv.append(c_new)
            rg_h.append(h_new)
        elif kind == 1:
            y, c_new, s_new = ssd_mixer(h, ssd_conv0[idx], ssd_s0[idx], P['ssd_w_in'][idx], P['ssd_conv_w'][idx],
                                        P['ssd_conv_b'][idx], P['ssd_dt_bias'][idx], P['ssd_a_log'][idx],
                                        P['ssd_d'][idx], P['ssd_norm_g'][idx], P['ssd_w_out'][idx])
            ssd_conv.append(c_new)
            ssd_s.append(s_new)
        else:
            y, s_new = hgrn2_mixer(h, hg_s0[idx], lower_bounds[layer], P['hg_w_in'][idx], P['hg_norm_g'][idx],
                                   P['hg_w_out'][idx])
            hg_s.append(s_new)
        x = x + rms_norm(y, g[1])
        h = rms_norm(x, g[2])
        y = memory_cross_attn(h, mem_k[layer], mem_v[layer], P['x_w_q'][layer], P['x_w_o'][layer])
        x = x + rms_norm(y, g[3])
    return x, jnp.stack(rg_conv), jnp.stack(rg_h), jnp.stack(ssd_conv), jnp.stack(ssd_s), jnp.stack(hg_s)

def setup_inputs(seed: int = 0) -> dict:
    key = jax.random.key(seed)
    keys = iter(jax.random.split(key, 48))

    def nrm(shape, scale):
        return scale * jax.random.normal(next(keys), shape, F32)

    def unif(shape, lo, hi):
        return jax.random.uniform(next(keys), shape, F32, lo, hi)

    d_in = D_MODEL ** -0.5
    lam_a = unif((N_A, LRU_WIDTH), 0.9, 0.999) ** (1.0 / LRU_C)
    dt0 = jnp.exp(unif((N_B, SSD_HEADS), float(np.log(1e-3)), float(np.log(1e-1))))
    return {
        'x_prompt': nrm((BATCH, SEQ, D_MODEL), 1.0),
        'x_sample': nrm((DEC_BATCH, DEC_SEQ, D_MODEL), 1.0),
        'mem_prompt': nrm((BATCH, N_MEM, D_MODEL), 1.0),
        'state_rglru_conv': nrm((N_A, DEC_BATCH, CONV_W - 1, LRU_WIDTH), 1.0),
        'state_rglru_h': nrm((N_A, DEC_BATCH, LRU_WIDTH), 0.5),
        'state_ssd_conv': nrm((N_B, DEC_BATCH, CONV_W - 1, SSD_CONV_DIM), 1.0),
        'state_ssd': nrm((N_B, DEC_BATCH, SSD_HEADS, SSD_HEAD_DIM, SSD_STATE), 0.1),
        'state_hgrn': nrm((N_C, DEC_BATCH, HGRN_HEADS, HGRN_KEY_DIM, HGRN_VAL_DIM), 0.3),
        'cache_mem_k': nrm((DEPTH, DEC_BATCH, N_MEM, X_HEADS, X_HEAD_DIM), 1.0),
        'cache_mem_v': nrm((DEPTH, DEC_BATCH, N_MEM, X_HEADS, X_HEAD_DIM), 1.0),
        'norm_g': 1.0 + nrm((DEPTH, 4, D_MODEL), 0.02),
        'mem_norm_g': 1.0 + nrm((DEPTH, D_MODEL), 0.02),
        'rg_w_in': nrm((N_A, D_MODEL, 2 * LRU_WIDTH), d_in),
        'rg_conv_w': nrm((N_A, CONV_W, LRU_WIDTH), CONV_W ** -0.5),
        'rg_conv_b': nrm((N_A, LRU_WIDTH), 0.01),
        'rg_w_a': nrm((N_A, LRU_BLOCKS, LRU_BLOCK, LRU_BLOCK), LRU_BLOCK ** -0.5),
        'rg_b_a': nrm((N_A, LRU_WIDTH), 0.01),
        'rg_w_x': nrm((N_A, LRU_BLOCKS, LRU_BLOCK, LRU_BLOCK), LRU_BLOCK ** -0.5),
        'rg_b_x': nrm((N_A, LRU_WIDTH), 0.01),
        'rg_lambda': jnp.log(lam_a) - jnp.log1p(-lam_a),
        'rg_w_out': nrm((N_A, LRU_WIDTH, D_MODEL), LRU_WIDTH ** -0.5),
        'ssd_w_in': nrm((N_B, D_MODEL, BRANCH + SSD_CONV_DIM + SSD_HEADS), d_in),
        'ssd_conv_w': nrm((N_B, CONV_W, SSD_CONV_DIM), CONV_W ** -0.5),
        'ssd_conv_b': nrm((N_B, SSD_CONV_DIM), 0.01),
        'ssd_dt_bias': dt0 + jnp.log(-jnp.expm1(-dt0)),
        'ssd_a_log': jnp.log(unif((N_B, SSD_HEADS), 1.0, 16.0)),
        'ssd_d': 1.0 + nrm((N_B, SSD_HEADS), 0.02),
        'ssd_norm_g': 1.0 + nrm((N_B, BRANCH), 0.02),
        'ssd_w_out': nrm((N_B, BRANCH, D_MODEL), BRANCH ** -0.5),
        'hg_w_in': nrm((N_C, D_MODEL, 4 * BRANCH), d_in),
        'hg_lower_bounds': nrm((DEPTH, BRANCH), 0.1),
        'hg_norm_g': 1.0 + nrm((N_C, BRANCH), 0.02),
        'hg_w_out': nrm((N_C, BRANCH, D_MODEL), BRANCH ** -0.5),
        'x_w_q': nrm((DEPTH, D_MODEL, D_MODEL), d_in),
        'x_w_k': nrm((DEPTH, D_MODEL, D_MODEL), d_in),
        'x_w_v': nrm((DEPTH, D_MODEL, D_MODEL), d_in),
        'x_w_o': nrm((DEPTH, D_MODEL, D_MODEL), d_in),
    }

def reference(x_prompt, x_sample, mem_prompt, state_rglru_conv, state_rglru_h, state_ssd_conv, state_ssd,
              state_hgrn, cache_mem_k, cache_mem_v, norm_g, mem_norm_g, rg_w_in, rg_conv_w, rg_conv_b, rg_w_a,
              rg_b_a, rg_w_x, rg_b_x, rg_lambda, rg_w_out, ssd_w_in, ssd_conv_w, ssd_conv_b, ssd_dt_bias,
              ssd_a_log, ssd_d, ssd_norm_g, ssd_w_out, hg_w_in, hg_lower_bounds, hg_norm_g, hg_w_out,
              x_w_q, x_w_k, x_w_v, x_w_o):
    P = {
        'norm_g': norm_g, 'rg_w_in': rg_w_in, 'rg_conv_w': rg_conv_w, 'rg_conv_b': rg_conv_b,
        'rg_w_a': rg_w_a, 'rg_b_a': rg_b_a, 'rg_w_x': rg_w_x, 'rg_b_x': rg_b_x, 'rg_lambda': rg_lambda,
        'rg_w_out': rg_w_out, 'ssd_w_in': ssd_w_in, 'ssd_conv_w': ssd_conv_w, 'ssd_conv_b': ssd_conv_b,
        'ssd_dt_bias': ssd_dt_bias, 'ssd_a_log': ssd_a_log, 'ssd_d': ssd_d, 'ssd_norm_g': ssd_norm_g,
        'ssd_w_out': ssd_w_out, 'hg_w_in': hg_w_in, 'hg_lower_bounds': hg_lower_bounds,
        'hg_norm_g': hg_norm_g, 'hg_w_out': hg_w_out, 'x_w_q': x_w_q, 'x_w_o': x_w_o,
    }
    dtype = x_prompt.dtype
    bp = x_prompt.shape[0]
    mem_kv = [memory_kv(mem_prompt, mem_norm_g[l], x_w_k[l], x_w_v[l]) for l in range(DEPTH)]
    new_mem_k_p = jnp.stack([kv[0] for kv in mem_kv])
    new_mem_v_p = jnp.stack([kv[1] for kv in mem_kv])
    y_prompt, rgc_p, rgh_p, sc_p, ss_p, hs_p = run_trunk(
        x_prompt, new_mem_k_p, new_mem_v_p,
        jnp.zeros((N_A, bp, CONV_W - 1, LRU_WIDTH), dtype),
        jnp.zeros((N_A, bp, LRU_WIDTH), dtype),
        jnp.zeros((N_B, bp, CONV_W - 1, SSD_CONV_DIM), dtype),
        jnp.zeros((N_B, bp, SSD_HEADS, SSD_HEAD_DIM, SSD_STATE), dtype),
        jnp.zeros((N_C, bp, HGRN_HEADS, HGRN_KEY_DIM, HGRN_VAL_DIM), dtype),
        P)
    y_sample, rgc_s, rgh_s, sc_s, ss_s, hs_s = run_trunk(
        x_sample, cache_mem_k, cache_mem_v, state_rglru_conv, state_rglru_h, state_ssd_conv, state_ssd,
        state_hgrn, P)
    return (y_prompt, y_sample, rgc_p, rgh_p, sc_p, ss_p, hs_p, new_mem_k_p, new_mem_v_p,
            rgc_s, rgh_s, sc_s, ss_s, hs_s)


_drawn_inputs = setup_inputs


def setup_inputs(seed=0):
    import zlib

    import numpy as np

    out = dict(_drawn_inputs(seed))
    spreads = {}
    factors = {'rg_b_a': 23.728,
     'rg_b_x': 8.0,
     'ssd_conv_b': 3.102,
     'ssd_d': 53.645,
     'ssd_norm_g': 27.085,
     'hg_norm_g': 48.93}
    for name, (base, spread) in spreads.items():
        noise = np.random.default_rng([zlib.crc32(name.encode()), seed]).standard_normal(out[name].shape)
        drawn = base * np.exp(spread * noise) if base else spread * noise
        out[name] = jnp.asarray(drawn.astype(out[name].dtype))
    for name, factor in factors.items():
        out[name] = (out[name] * factor).astype(out[name].dtype)
    return out
```

```python
from contextlib import ExitStack

import concourse.bass as bass
from concourse import mybir

F32 = mybir.dt.float32
F32R = mybir.dt.float32r
ALU = mybir.AluOpType
ACT = mybir.ActivationFunctionType
AX = mybir.AxisListType.X

P = 128
D = 1024
KD = D // P
BR = 2 * D
SEQ = 256
NB = 8
NL = 8
NS = NB * NL
NT = SEQ + NS
DEPTH = 4
NMEM = 256
XH = 4
EPS = 1e-6
GROUPS = 8
SEG = NL + 3
EXT = SEQ + 3 + NB * SEG
CV = EXT - 3
SC = SEQ + 3
SLOTS = 4
RG_STEPS, SSD_STEPS, HG_STEPS = 9, 3, 8
RG_DVE, SSD_DVE, HG_DVE = 21, 49, 33
TINY = 2.0 ** -60
SIG_SET = "sigmoid_and_others"
EXP_SET = "natural_log_exp_and_others"

MIX_UNITS, ATT_UNITS, OUT_UNITS = 8 * GROUPS, 32, 16
MIX_AT = [0, 96, 192, 304]
OUT_AT = 256
ATT_AT = [64, 160, 272, 368]
N_UNITS = 400


class Count:

    def __init__(self, n=0):
        self.n, self.i = n, None

    def enter(self, i, i0, per):
        self.i, self.i0, self.per, self.n0 = i, i0, per, self.n

    def leave(self, times):
        assert self.n == self.n0 + self.per, ("counted", self.n - self.n0, "stated", self.per)
        self.n, self.i = self.n0 + times * self.per, None

    def at(self, d=0):
        if self.i is None:
            return self.n + d
        return self.i * self.per + (self.n + d - self.i0 * self.per)


class Chain:

    def __init__(self, eng, sem):
        self.eng, self.sem, self.count = eng, sem, Count()

    def did(self, ins):
        ins.then_inc(self.sem, 1)
        self.count.n += 1

    def sync(self):
        self.eng.wait_ge(self.sem, self.count.at())


def first(i):
    return isinstance(i, int)


def trunk(nc, A, OUT):
    with ExitStack() as ctx:
        def sb(name, shape, dt=F32):
            return ctx.enter_context(nc.sbuf_tensor(name, shape, dt))

        sems = {}

        shared = {"lam_abs": ("par_read", 1, 2), "lb_diff": ("par_read", 1, 3), "sd_wdt": ("par_read", 1, 4),
                  "sd_dt_abs": ("par_read", 1, 5), "sd_dta": ("par_read", 1, 6),
                  "lb_exp": ("lam_exp", 1, 1), "sd_wdt_high": ("lam_exp", 1, 2), "sd_dt_exp": ("lam_exp", 1, 3),
                  "sd_a": ("lam_exp", 1, 4), "sd_sums_read": ("lam_exp", 1, 5),
                  "sd_dt_full": ("pro_full", 1, 18), "sd_sums_full": ("pro_full", 1, 19), "yt_full": ("pro_full", 1, 20),
                  "hg_s0_in": ("sd_s0_in", 1, 32 * GROUPS), "hg_stored": ("sd_stored", 1, 48 * GROUPS)}
        for what, n in (("sn{}_full", 4), ("sn{}_read", 4), ("st{}_full", 4), ("st{}_read", 4), ("seg{}_full", 3),
                        ("seg{}_ready", 3), ("exp{}", 3), ("y{}_full", 2), ("y{}_read", 2)):
            for k in range(n):
                shared["sd_" + what.format(k)] = ("sd_" + what.format("s"), n, k + 1 - n)
        for hgrn, ssd_ in (("D_ready", "bt_full"), ("G_ready", "bt_read"), ("K_ready", "cb_full"), ("att_full", "cb_read"),
                           ("att_ready", "conv_done"), ("exps", "eo_full"), ("f_read", "eo_read"), ("forget", "f_ready"),
                           ("g_read", "ht_full"), ("g_sig", "ht_read"), ("kt_full", "in_read"), ("kt_read", "in_ready"),
                           ("logf", "m_ready"), ("o_full", "o_high"), ("o_read", "o_ready"), ("o_ready", "rs_ready"),
                           ("osq_ready", "s1_full"), ("q_read", "s1_read"), ("q_sig", "sf_full"), ("rs_ready", "sf_read"),
                           ("s1_full", "sig_ready"), ("s1_read", "so_full"), ("s2_full", "so_ready"), ("sf_read", "ssq_full"),
                           ("sn_full", "xs_full"), ("sn_read", "xs_read"), ("ssq_full", "xt_full"), ("v_read", "xt_read"),
                           ("vm_ready", "xw_ready")):
            shared["hg_" + hgrn] = ("sd_" + ssd_, 1, GROUPS)

        def past(name, n):
            _, scale, base = shared.get(name, (name, 1, 0))
            if scale > 1:
                n = n * scale
            return S(name), (n + base if base else n)

        def S(name):
            name = shared.get(name, (name,))[0]
            if name not in sems:
                sems[name] = ctx.enter_context(nc.semaphore(name))
            return sems[name]

        X = sb("X", [P, KD, NT])
        Hh, Hl = sb("Hh", [P, KD, NT], F32R), sb("Hl", [P, KD, NT], F32R)
        memn = sb("memn", [P, KD, NMEM])
        raw = sb("raw", [P, SLOTS, 8, 256])
        wh, wl = sb("wh", [P, 2, 8, P], F32R), sb("wl", [P, 2, 8, P], F32R)
        ident, ones, upper = sb("ident", [P, P]), sb("ones", [P, P]), sb("upper", [P, P])
        later = sb("later", [P, P])
        s_causal = sb("s_causal", [P, NS])
        s_later = sb("s_later", [P, NS])
        s_block = sb("s_block", [P, NB])
        restart = sb("restart", [P, NT])
        par = sb("par", [P, 6, P])
        smallc = sb("smallc", [P, 512])
        rs = sb("rs", [P, NT])
        wdth, wdtl = sb("wdth", [P, KD, 32], F32R), sb("wdtl", [P, KD, 32], F32R)
        dmask = sb("dmask", [P, 72])
        with ExitStack() as layout:
            def lay(name, shape, dt=F32):
                return layout.enter_context(nc.sbuf_tensor(name, shape, dt))
            Oh16, Ol16 = lay("Oh16", [P, 16, NT], F32R), lay("Ol16", [P, 16, NT], F32R)
            hg_osq, hg_rs = lay("hg_osq", [P, 2, NT])[:], lay("hg_rs", [P, 2, NT])[:]
        Oh, Ol = sb("Oh", [P, KD, NT], F32R), sb("Ol", [P, KD, NT], F32R)
        WORK2 = 2 * KD * NT
        work2 = sb("work2", [P, WORK2])
        ug = sb("ug", [P, 2, 2, CV + 1], F32R)
        WORK = 15984
        work = sb("work", [P, WORK])
        ps = ctx.enter_context(nc.psum_tensor("ps", [P, 8, 512], F32))

        def carver(start, work=work, WORK=WORK):
            at = [start]

            def carve(*shape):
                n = 1
                for s in shape:
                    n *= s
                v = work[:, at[0]:at[0] + n]
                at[0] += n
                assert at[0] <= WORK, at[0]
                if len(shape) == 2:
                    v = v.rearrange("p (a b) -> p a b", a=shape[0])
                if len(shape) == 3:
                    v = v.rearrange("p (a b c) -> p a b c", a=shape[0], b=shape[1])
                return v
            return carve

        carve = carver(0)
        Y, SQ = carve(KD, NT), carve(KD, NT)

        eps_c, tiny_c, zero_c = smallc[:, 0:1], smallc[:, 1:2], smallc[:, 2:3]
        lb, oml = smallc[:, 176:192], smallc[:, 192:208]
        dcol = smallc[:, 208:224]
        rgc = smallc[:, 16:176].rearrange("p (c l t) -> p c l t", c=5, l=2)
        dtb, alog = smallc[:, 224:256], smallc[:, 256:288]

        landed = [S(f"w_landed{s}") for s in range(SLOTS)]
        hi_ready, lo_ready, used = S("w_hi_ready"), S("w_lo_ready"), S("w_used")

        def after(stage, i, i0, what):
            if stage == "hg":
                return MIX_AT[2] + 8 * (i - i0) + {"g": 2, "q": 4, "f": 6, "v": 8}[what]
            base = {("rg", 0): MIX_AT[0], ("rg", 8): MIX_AT[3], ("ssd", 0): MIX_AT[1]}[stage, i0]
            firsts = {"rg": {"u": 2, "g": 4, "r": 6}, "ssd": {"bc": 2, "x": 4, "z": 6}}[stage]
            later_ = {"rg": {"u": 0, "g": 2, "out": 4, "r": 6}, "ssd": {"bc": 0, "x": 2, "z": 4, "out": 6}}[stage]
            if first(i) and i == i0:
                return base + firsts[what]
            return (i - i0) * 8 + (base + later_[what])

        def cols_of(w, c0):
            v = w.rearrange("(k p) n -> p k n", p=P)
            return lambda dst, q: (dst[:, 2 * q:2 * q + 2, :], v[:, 2 * q:2 * q + 2, bass.ds(c0, 256)])

        def pair_of(w, c0, c1):
            v = w.rearrange("(k p) n -> p k n", p=P)

            def f(dst, q):
                h, k = q // 2, 4 * (q % 2)
                return dst[:, k:k + 4, h * P:(h + 1) * P], v[:, k:k + 4, bass.ds((c0, c1)[h], P)]
            return f

        def rows_of(w, r0):
            def f(dst, q):
                k, c = q // 2, 512 * (q % 2)
                return (dst[:, 2 * q:2 * q + 2, :],
                        w[bass.ds(r0 + k * P, P), c:c + 512].rearrange("p (q c) -> p q c", q=2))
            return f

        def gates_of(wa, wx, g):
            def f(dst, q):
                h, k = q // 2, q % 2
                src = (wa, wx)[h].rearrange("g i (j c) -> (g i) j c", c=P)[bass.ds(g * 256 + k * P, P)]
                return dst[:, 2 * k:2 * k + 2, h * P:(h + 1) * P], src
            return f

        lam_e, lb_e, tmp32 = smallc[:, 352:384], smallc[:, 384:448], smallc[:, 448:512]
        hg_gt = sb("hg_gt", [P, 2, 40])
        hg_B, hg_A, hg_eA = sb("hg_B", [P, 4, 8])[:], sb("hg_A", [P, 4, 9])[:], sb("hg_eA", [P, 4, 9])[:]
        hg_eg, hg_en, hg_cur = sb("hg_eg", [P, 2, 8])[:], sb("hg_en", [P, 2, 8])[:], sb("hg_cur", [P, 3, 2])[:]

        def samples(v, c0):
            return v[:, :, c0:c0 + NB * SEG].rearrange("p t (b s) -> p t b s", b=NB)

        Y_DONE = [64, 128, 136, 200]

        w_rg = lambda l: A["rg_w_in"][l]
        w_ssd, w_hg = A["ssd_w_in"][0], A["hg_w_in"][0]

        block = ctx.enter_context(nc.Block())

        c = carver(2 * KD * NT)
        x_rows, mem_rows, par_rows = c(3, D), c(2, D), c(6, P)
        tm = c(6, P)

        c = carver(KD * NT)
        rg_in = c(2, EXT)
        rg_u, rg_r, rg_i, rg_t, rg_a = c(2, EXT), c(2, EXT), c(2, EXT), c(2, EXT), c(2, EXT)
        rg_gate, rg_o = c(2, NT), c(2, NT)
        rg_h0, rg_pack, rg_so, rg_cur, rg_hist, rg_fix = c(2, NB), c(2, 36), c(2, P), c(9, 2), c(2, P), c(2, NB)

        c = carver(KD * NT)
        sd_in, sd_c = c(4, EXT), c(4, EXT)
        d = carver(KD * NT + 4 * EXT)
        sd_yo2, sd_yo, sd_rs = d(2, NT), d(2, 192), d(NT)
        sd_f, sd_z = c(4, NT), c(2, NT)
        sd_sig = sd_f
        sd_xt, sd_xw = c(3, 4, 64), c(3, 4, 64)
        sd_xf, sd_bt, sd_bm = c(4, 64), c(3, P), c(NB, P)
        sd_cb, sd_e = c(3, P), c(3, 4, P)
        sd_eo, sd_s0 = c(2, 200), c(2, NB, P)
        sd_tc = c(5, 3, 4)
        sd_cur = c(7, 4)
        c = carver(0, work2, WORK2)
        sd_st = c(2, NB, P)
        sd_s1, sd_sf = c(2, P), c(2, P)
        sd_y, wdt = c(2, NT), c(KD, 32)
        sd_hist, sd_pack, sd_so = c(4, P), c(4, 27), c(4, P)
        sd_ta = c(5, 3, 32)
        sd_tw = sd_xt.rearrange("p a b c -> p (a b c)")[:, 0:576].rearrange("p (a b) -> p a b", b=96)
        c = carver(0)
        hg_s0 = c(2, NB, P)
        hg_g, hg_q, hg_f, hg_k, hg_G, hg_x = c(2, NT), c(2, NT), c(2, NT), c(2, NT), c(2, NT), c(2, NT)
        hg_v, hg_vm, hg_kt = c(3, 256), c(NB, 256), c(3, P)
        hg_D = c(4, 72)
        hg_K = [c(9, P), c(9, P), c(9, P), c(9, P)]
        hg_ks = c(2, NS)
        hg_att = [c(NT), c(NT)]
        hg_s1, hg_sf, hg_o = c(2, P), c(2, P), c(2, NT)

        c = carver(0)
        at_kbt = c(2, KD, P)
        at_ppt = work[:, 0:2048].rearrange("p (h a m) -> p h a m", h=XH, a=2)
        at_so = c(2, 256)
        at_p, at_pp, kb3 = c(2, 256), c(XH, 256), c(D)
        at_k, at_v, at_kt, at_q = c(2, 2, 256), c(2, D), c(KD, 256), c(KD, NT)
        at_vt = at_q
        at_qz = work[:, 2048:4096].rearrange("p (b c q) -> p b c q", b=NB, c=KD)
        at_ptz = at_kt.rearrange("p k m -> p (k m)").rearrange("p (a b h q) -> p a b h q", a=2, b=NB, h=XH)
        memh = work[:, WORK - 3072:WORK - 1024].rearrange("p (k m) -> p k m", k=KD)
        c = carver(WORK - 3072)
        at_kb = [c(D), c(D), c(D), kb3]
        at_m = smallc[:, 288:352].rearrange("p (a b) -> p a b", b=8)

        @block.sync
        def _(sp):
            blocks = Count()

            def put(load):
                m = blocks.n
                slot = m % SLOTS
                if m >= SLOTS:
                    sp.wait_ge(lo_ready, blocks.at() * 2 - 2 * (SLOTS - 1))
                for q in (1, 2, 3, 0):
                    dst, src = load(raw[:, slot], q)
                    sp.dma_start(dst, src).then_inc(landed[slot], 16)
                blocks.n += 1

            rows = [("norm_g", "l j (t c) -> (l j t) c", 0, 0), ("rg_conv_w", "l k (t c) -> (l k t) c", 1, 0),
                    ("rg_conv_b", "l (t c) -> (l t) c", 2, 0), ("rg_b_a", "l (t c) -> (l t) c", 2, 32),
                    ("rg_b_x", "l (t c) -> (l t) c", 2, 64), ("rg_lambda", "l (t c) -> (l t) c", 2, 96),
                    ("ssd_conv_w", "l k (t c) -> (l k t) c", 3, 0), ("ssd_conv_b", "l (t c) -> (l t) c", 4, 0),
                    ("ssd_norm_g", "l (t c) -> (l t) c", 4, 32), ("hg_norm_g", "l (t c) -> (l t) c", 4, 48),
                    ("hg_lower_bounds", "l (t c) -> (l t) c", 4, 64), ("mem_norm_g", "l (t c) -> (l t) c", 5, 0)]
            sp.dma_start(x_rows[:, 0:2, :], A["x_prompt"][0].rearrange("(a p) d -> p a d", p=P)).then_inc(S("in_x"), 16)
            sp.dma_start(x_rows[64:128, 2, :], A["x_sample"].rearrange("b l d -> (b l) d")).then_inc(S("in_x"), 16)
            sp.dma_start(x_rows[0:64, 2, :], A["x_sample"].rearrange("b l d -> (b l) d")).then_inc(S("in_x"), 16)
            for name, how, tile, r0 in rows:
                src = A[name].rearrange(how, c=P)
                sp.dma_start(par_rows[r0:r0 + src.shape[0], tile, :], src).then_inc(S("in_par"), 16)
            with nc.allow_non_contiguous_dma(reason="32 values, spread over the partitions"):
                d = A["ssd_d"].rearrange("l (t h) -> l h t", h=2)
                for h in range(2):
                    sp.dma_start(dcol[64 * h:64 * h + 64, :], d[0:1, h, :].broadcast_to([64, 16])).then_inc(S("in_head"), 16)
            sp.dma_start(dtb, A["ssd_dt_bias"][0:1, :].broadcast_to([P, 32])).then_inc(S("in_head"), 16)
            sp.dma_start(alog, A["ssd_a_log"][0:1, :].broadcast_to([P, 32])).then_inc(S("in_head"), 16)
            for j in range(2):
                sp.dma_start(mem_rows[:, j, :], A["mem_prompt"][0, j * P:(j + 1) * P, :]).then_inc(S("in_mem"), 16)
            sp.wait_ge(*past("raw_clear", 1))

            def two_peeled(i0, body):
                body(i0)
                body(i0 + 1)
                with sp.Fori(i0 + 2, i0 + GROUPS) as i:
                    blocks.enter(i, i0 + 2, 4)
                    body(i)
                    blocks.leave(GROUPS - 2)

            def rg_store(l, i):
                c0 = (i - 8 * l) * 256
                cols = bass.ds(c0, 256)
                sp.wait_ge(*past("rg_so_ready", i + 1))
                flat = rg_so.rearrange("p t c -> p (t c)")
                for o, n, r in ((OUT["rgc_p"][l, 0, :, cols], 3, 0),
                                (OUT["rgc_s"][l].rearrange("b k c -> (b k) c")[:, cols], 24, 3),
                                (OUT["rgh_p"][l, :, cols], 1, 27), (OUT["rgh_s"][l, :, cols], 8, 28)):
                    sp.dma_start(o, flat[r:r + n, :]).then_inc(S("rg_stored"), 16)

            def rg(l):
                i0 = 8 * l
                wa, wx = A["rg_w_a"][l], A["rg_w_x"][l]

                def hist(i):
                    cols = bass.ds((i - i0) * 256, 256)
                    if i0 or not first(i) or i > 0:
                        sp.wait_ge(*past("rg_ht_full", i))
                    flat = rg_hist.rearrange("p t c -> p (t c)")
                    sp.dma_start(flat[0:24, :], A["state_rglru_conv"][l].rearrange("b k c -> (b k) c")[:, cols]).then_inc(S("rg_hist_in"), 16)
                    sp.dma_start(flat[24:32, :], A["state_rglru_h"][l][:, cols]).then_inc(S("rg_hist_in"), 16)

                def body(i):
                    c0 = (i - i0) * 256
                    put(cols_of(w_rg(l), c0))
                    put(cols_of(w_rg(l), c0 + BR))
                    if not (first(i) and i == i0):
                        hist(i)
                        put(rows_of(A["rg_w_out"][l], c0 - 256))
                    put(gates_of(wa, wx, i - i0))
                    if first(i) and i == i0:
                        sp.wait_ge(*past("h_ready", KD * (1 if l == 0 else 10)))
                        hist(i)
                    elif not first(i):
                        rg_store(l, i - 2)
                two_peeled(i0, body)
                put(rows_of(A["rg_w_out"][l], 7 * 256))
                rg_store(l, i0 + 6)
                rg_store(l, i0 + 7)

            def ssd():
                st = A["state_ssd"][0].rearrange("b (g t h) p n -> g t (h p) b n", t=2, h=2)
                so = OUT["ss_s"][0].rearrange("b (g t h) p n -> g t (h p) b n", t=2, h=2)
                sq = OUT["ss_p"][0, 0].rearrange("(g t h) p n -> g (h p) t n", t=2, h=2)

                def one(v, i):
                    return v[bass.ds(i, 1)]

                def load(i):
                    if not first(i) or i > 0:
                        sp.wait_ge(*past("sd_stored", i * 48))
                    for t in range(2):
                        sp.dma_start(sd_s0[:, t], one(st, i)[0, t]).then_inc(S("sd_s0_in"), 16)

                def store(i):
                    sp.wait_ge(*past("sd_so_ready", i + 1))
                    sp.wait_ge(*past("sd_sf_read", i + 1))
                    for t in range(2):
                        sp.dma_start(one(so, i)[0, t], sd_s0[:, t]).then_inc(S("sd_stored"), 16)
                    sp.dma_start(one(sq, i)[0], sd_sf).then_inc(S("sd_stored"), 16)
                    flat = sd_so.rearrange("p t c -> p (t c)")
                    for c0, n, at in ((BR + i * P, P, 0), (BR + 1024 + i * P, P, P), (i * 256, 256, 256)):
                        sp.dma_start(OUT["sc_p"][0, 0][:, bass.ds(c0, n)], flat[0:3, at:at + n]).then_inc(S("sd_so_out"), 16)
                        sp.dma_start(OUT["sc_s"][0].rearrange("b k c -> (b k) c")[:, bass.ds(c0, n)], flat[3:27, at:at + n]).then_inc(S("sd_so_out"), 16)

                def hist(i):
                    if not first(i) or i > 0:
                        sp.wait_ge(*past("sd_ht_full", i))
                    flat = sd_hist.rearrange("p t c -> p (t c)")
                    for c0, n, at in ((BR + i * P, P, 0), (BR + 1024 + i * P, P, P), (i * 256, 256, 256)):
                        sp.dma_start(flat[0:24, at:at + n], A["state_ssd_conv"][0].rearrange("b k c -> (b k) c")[:, bass.ds(c0, n)]).then_inc(S("sd_hist_in"), 16)

                def body(i):
                    put(pair_of(w_ssd, i * P + 2 * BR, i * P + 2 * BR + 1024))
                    put(cols_of(w_ssd, i * 256 + BR))
                    if not (first(i) and i == 0):
                        hist(i)
                    if not first(i):
                        store(i - 2)
                        load(i - 1)
                    put(cols_of(w_ssd, i * 256))
                    if first(i) and i == 0:
                        sp.wait_ge(*past("h_ready", 4 * KD))
                        sp.dma_start(wdt, w_ssd.rearrange("(k p) n -> p k n", p=P)[:, :, BR + 4096:]).then_inc(S("in_wdt"), 16)
                        hist(0)
                        load(0)
                    else:
                        put(rows_of(A["ssd_w_out"][0], i * 256 - 256))
                two_peeled(0, body)
                put(rows_of(A["ssd_w_out"][0], 7 * 256))
                store(6)
                load(7)
                store(7)

            def hg():
                st = A["state_hgrn"][0].rearrange("b (g t) k v -> g t k b v", t=2)
                so = OUT["hs_s"][0].rearrange("b (g t) k v -> g t k b v", t=2)
                sq = OUT["hs_p"][0, 0].rearrange("(g t) k v -> g k t v", t=2)

                def load(i):
                    if not first(i) or i > 0:
                        sp.wait_ge(*past("hg_stored", i * 48))
                    for t in range(2):
                        sp.dma_start(hg_s0[:, t], st[bass.ds(i, 1)][0, t]).then_inc(S("hg_s0_in"), 16)

                def store(i):
                    sp.wait_ge(*past("hg_sn_read", i * 4 + 4))
                    sp.wait_ge(*past("hg_sf_read", i * 2 + 2))
                    for t in range(2):
                        sp.dma_start(so[bass.ds(i, 1)][0, t], hg_s0[:, t]).then_inc(S("hg_stored"), 16)
                    sp.dma_start(sq[bass.ds(i, 1)][0], hg_sf).then_inc(S("hg_stored"), 16)

                def body(i):
                    put(cols_of(w_hg, i * 256 + 3 * BR))
                    put(cols_of(w_hg, i * 256))
                    if not first(i):
                        store(i - 2)
                        load(i - 1)
                    put(cols_of(w_hg, i * 256 + BR))
                    put(cols_of(w_hg, i * 256 + 2 * BR))
                    if first(i) and i == 0:
                        sp.wait_ge(*past("h_ready", 7 * KD))
                        load(0)
                two_peeled(0, body)
                w = A["hg_w_out"][0]
                for c in range(4):
                    for kc in range(2):
                        put(cols_of(w[kc * D:(kc + 1) * D, :], c * 256))
                    if c == 0:
                        store(6)
                        load(7)
                    if c == 1:
                        store(7)

            def attention(layer):
                for name in ("x_w_k", "x_w_v"):
                    for h in range(XH):
                        put(cols_of(A[name][layer], h * 256))
                        if name == "x_w_v":
                            sp.wait_ge(*past("at_k_ready", layer * XH + h + 1))
                            sp.dma_start(OUT["mk"][layer, 0, :, h, :].rearrange("(a p) d -> p a d", p=P), at_k[:, h % 2]).then_inc(S(f"at_k_out{h % 2}"), 16)
                seen = layer * 2 * NB * 2

                def cache(n):
                    b, half = n % 16 // 2, n % 2
                    src = A["cache_mem_k" if n < 16 else "cache_mem_v"][layer, b, half * P:(half + 1) * P].rearrange("m h d -> m (h d)")
                    if n >= 4 or layer:
                        sp.wait_ge(*past("at_kb_used", seen + n - 3))
                    sp.dma_start(at_kb[n % 4], src).then_inc(S(f"at_kb_in{n % 4}"), 16)
                for h in range(4):
                    put(cols_of(A["x_w_q"][layer], h * 256))
                sp.wait_ge(*past("at_area", layer + 1))
                for n in range(4):
                    cache(n)
                sp.wait_ge(*past("at_v_ready", layer * XH + XH))
                sp.dma_start(OUT["mv"][layer, 0].rearrange("(a p) h d -> p a (h d)", p=P), at_v).then_inc(S("at_v_out"), 16)
                for h in range(4):
                    put(cols_of(A["x_w_o"][layer], h * 256))
                for n in range(4, 32):
                    cache(n)

            rg(0)
            attention(0)
            ssd()
            attention(1)
            hg()
            attention(2)
            rg(1)
            attention(3)
            sp.wait_ge(*past("y_ready", 1))
            sp.dma_start(OUT["y_p"][0].rearrange("(a p) d -> p a d", p=P), x_rows[:, 0:2, :]).then_inc(S("out_y"), 16)
            sp.dma_start(OUT["y_s"].rearrange("b l d -> (b l) d"), x_rows[64:128, 2, :]).then_inc(S("out_y"), 16)
            sp.wait_ge(*past("out_y", 32))
            sp.wait_ge(*past("rg_stored", 2 * GROUPS * 64))
            sp.wait_ge(*past("sd_stored", GROUPS * 48))
            sp.wait_ge(*past("sd_so_out", GROUPS * 96))
            sp.wait_ge(*past("hg_stored", GROUPS * 48))
            for h in range(2):
                sp.wait_ge(*past(f"at_k_out{h}", DEPTH * 2 * 16))
            sp.wait_ge(*past("at_v_out", DEPTH * 16))

        @block.tensor
        def _(pe):
            units = Count()
            fresh = []

            def halves(n=1):
                pe.wait_ge(hi_ready, units.at(n))
                pe.wait_ge(lo_ready, units.at(n))

            def done(mm, n=1):
                mm.then_inc(used, n)
                units.n += n

            def three(out, wi, mh, ml, start, stop):
                pe.matmul(out, wh[:, wi[0], wi[1]], mh, start=start, stop=False)
                pe.matmul(out, wh[:, wi[0], wi[1]], ml, start=False, stop=False)
                return pe.matmul(out, wl[:, wi[0], wi[1]], mh, start=False, stop=stop)

            def project(bank, half, mh=Hh, ml=Hl, n=NT):
                pe.wait_ge(hi_ready, units.at(1))
                for k in range(8):
                    if fresh:
                        pe.wait_ge(*past("h_ready", fresh[0] + k + 1))
                    pe.matmul(ps[:, bank, 0:n], wh[:, half, k], mh[:, k, 0:n], start=(k == 0), stop=False)
                    pe.matmul(ps[:, bank, 0:n], wh[:, half, k], ml[:, k, 0:n], start=False, stop=False)
                fresh.clear()
                pe.wait_ge(lo_ready, units.at(1))
                for k in range(8):
                    mm = pe.matmul(ps[:, bank, 0:n], wl[:, half, k], mh[:, k, 0:n], start=False, stop=(k == 7))
                done(mm)

            def project_rows(half, tiles, bank, wait_read):
                halves()
                for q in range(4):
                    t = 4 * half + q
                    wait_read(t)
                    for k in range(2):
                        mm = three(ps[:, bank(t), 0:NT], (half, 4 * k + q), Oh[:, k, :], Ol[:, k, :], k == 0, k == 1)
                    if q < 3:
                        mm.then_inc(S("out_full"), 1)
                done(mm)

            def sum_squares(n, bank, width=NT):
                for k in range(KD):
                    pe.wait_ge(*past("sq_ready", n * KD + k + 1))
                    mm = pe.matmul(ps[:, bank, 0:width], ones[:], SQ[:, k, 0:width], start=(k == 0), stop=(k == KD - 1))
                mm.then_inc(S("ssq_full"), 1)

            pe.wait_ge(*past("consts", 1))
            items = [[par_rows[:, t, :] for t in range(4)], [par_rows[:, 4, :], par_rows[0:32, 5, :]]]
            items += [[x_rows[:, a, k * P:(k + 1) * P] for a in range(3)] for k in range(KD)]
            items += [[mem_rows[:, a, k * P:(k + 1) * P] for a in range(2)] for k in range(KD)]
            pe.wait_ge(*past("in_par", 16 * 12))
            for n, tiles in enumerate(items):
                if n == 2:
                    pe.wait_ge(*past("in_x", 48))
                if n == 10:
                    pe.wait_ge(*past("in_mem", 32))
                if n in (8, 9):
                    pe.wait_ge(*past("par_read", n - 7))
                if n >= 10:
                    pe.wait_ge(*past("x_ready", n - 9))
                for j, tile in enumerate(tiles):
                    r = tile.shape[0]
                    mm = pe.transpose(ps[:, n % 8, j * P:j * P + r], tile, ident[0:r, 0:r])
                mm.then_inc(S("pro_full"), 1)
            pe.wait_ge(*past("mem_ready", KD))
            sum_squares(0, 6, NMEM)
            sum_squares(1, 7)

            def rg(l):
                i0 = 8 * l

                def take_u(i):
                    if not (i0 == 0 and first(i) and i == 0):
                        pe.wait_ge(*past("rg_conv_done", i))
                    project(0, 0)
                    pe.wait_ge(*past("rg_hist_in", 32 * (i + 1) if first(i) else i * 32 + 32))
                    project(1, 1)
                    for t in range(2):
                        mm = pe.transpose(ps[:, 1, 320 + 32 * t:352 + 32 * t], rg_hist[0:32, t, :], ident[0:32, 0:32])
                    mm.then_inc(S("rg_ht_full"), 1)

                def take_gate(i):
                    if not (i0 == 0 and first(i) and i == 0):
                        pe.wait_ge(*past("rg_in_read", i))
                    project(2, 0)
                    project(3, 1)

                def take_out(i, after=2):
                    pe.wait_ge(*past("rg_pack_ready", i + 1))
                    pe.wait_ge(*past("rg_o_ready", i + 1))

                    def wait_read(t):
                        if t < 4:
                            if t == 0:
                                pe.wait_ge(*past("rg_ri_read", i + 1))
                        else:
                            pe.wait_ge(*past("y_added", y_count(i, t - 3)))
                    project_rows(0, None, lambda t: 4 + t % 4, wait_read)
                    pe.wait_ge(*past("rg_gate_read", i + after))
                    project_rows(1, None, lambda t: 4 + t % 4, wait_read)
                    for t in range(2):
                        mm = pe.transpose(ps[0:36, 2 + t, 320:448], rg_pack[:, t, :], ident[:])
                    mm.then_inc(S("rg_so_full"), 1)

                def y_count(i, n):
                    base = 0 if l == 0 else Y_DONE[2]
                    return (i - i0) * 8 + (base + n)

                def take_ri(i):
                    pe.wait_ge(*past("rg_u_ready", i + 1))
                    if not (first(i) and i == i0):
                        pe.wait_ge(*past("y_added", y_count(i - 1, 8)))
                    for m in range(2):
                        pe.wait_ge(hi_ready, units.at(1))
                        for j in range(2):
                            for k in range(2):
                                for part in range(2):
                                    pe.matmul(ps[:, 4 + 2 * m + j, 0:CV], wh[:, m, 2 * k + j], ug[:, part, k, 0:CV], start=(k == 0 and part == 0), stop=False)
                        pe.wait_ge(lo_ready, units.at(1))
                        for j in range(2):
                            for k in range(2):
                                mm = pe.matmul(ps[:, 4 + 2 * m + j, 0:CV], wl[:, m, 2 * k + j], ug[:, 0, k, 0:CV], start=False, stop=(k == 1))
                        done(mm)

                fresh.append(KD * (0 if l == 0 else 9))
                take_u(i0)
                take_gate(i0)
                take_ri(i0)
                with pe.Fori(i0 + 1, i0 + GROUPS) as i:
                    units.enter(i, i0 + 1, 8)
                    take_u(i)
                    take_gate(i)
                    take_out(i - 1)
                    take_ri(i)
                    units.leave(GROUPS - 1)
                take_out(i0 + 7, 1)

            def ssd():
                pe.wait_ge(*past("h_ready", 4 * KD))
                pe.wait_ge(*past("sd_wdt", 1))
                for T in range(3):
                    t0 = (0, P, NT - P)[T]
                    for k in range(KD):
                        for n, (x, w) in enumerate(((Hh, wdth), (Hh, wdtl), (Hl, wdth))):
                            mm = pe.matmul(ps[:, 0, 32 * T:32 * T + 32], x[:, k, t0:t0 + P], w[:, k, :],
                                           start=(k == 0 and n == 0), stop=(k == KD - 1 and n == 2))
                mm.then_inc(S("sd_dt_full"), 1)
                pe.wait_ge(*past("sd_dta", 1))
                for T in range(2):
                    pe.matmul(ps[:, 1, 32 * T:32 * T + 32], upper[:], sd_ta[:, 1, T, :], start=True, stop=True)
                    pe.matmul(ps[:, 1, 96 + 32 * T:128 + 32 * T], later[:], sd_ta[:, 1, T, :], start=True, stop=True)
                pe.matmul(ps[:, 1, 192:224], ones[:], sd_ta[:, 1, 1, :], start=True, stop=True)
                pe.matmul(ps[64:P, 1, 64:96], s_causal[64:P], sd_ta[64:P, 1, 2, :], start=True, stop=True)
                pe.matmul(ps[64:P, 1, 160:192], s_later[64:P], sd_ta[64:P, 1, 2, :], start=True, stop=True).then_inc(S("sd_sums_full"), 1)
                pe.wait_ge(*past("sd_sums_read", 1))

                def take_bc(i):
                    if not first(i):
                        pe.wait_ge(*past("sd_z_read", i))
                    elif i > 0:
                        pe.wait_ge(*past("sd_z_read", i))
                    project(0, 0)
                    pe.wait_ge(*past("sd_hist_in", i * 48 + 48))
                    project(1, 1)
                    for t in range(4):
                        mm = pe.transpose(ps[:, 1, 320 + 24 * t:344 + 24 * t], sd_hist[0:24, t, :], ident[0:24, 0:24])
                    mm.then_inc(S("sd_ht_full"), 1)

                def take_x(i, half):
                    if half == 0 and not (first(i) and i == 0):
                        pe.wait_ge(*past("sd_in_ready", i))
                    project(2 + half, half)

                def take_z(i):
                    pe.wait_ge(*past("sd_in_ready", i + 1))
                    pe.wait_ge(*past("sd_ht_read", i + 1))
                    project(0, 0)
                    project(1, 1)

                def mix1(i):
                    pe.wait_ge(*past("sd_f_ready", i + 1))
                    pe.wait_ge(*past("y_added", i * 8 + Y_DONE[0]))
                    for T in range(2):
                        for j in range(2):
                            mm = pe.transpose(ps[:, 4, (2 * T + j) * P:(2 * T + j + 1) * P], sd_f[:, 2 + j, T * P:(T + 1) * P], ident[:])
                    mm.then_inc(S("sd_xt_full"), 1)
                    for j in range(3):
                        mm = pe.transpose(ps[:, 5, j * P:(j + 1) * P], sd_f[:, (2, 3, 0)[j], NT - P:NT], ident[:])
                    mm.then_inc(S("sd_xs_full"), 1)
                    for T in range(2):
                        mm = pe.transpose(ps[:, 6, T * P:(T + 1) * P], sd_f[:, 0, T * P:(T + 1) * P], ident[:])
                    mm.then_inc(S("sd_bt_full"), 1)
                    for T in range(2):
                        pe.matmul(ps[:, 7, T * P:(T + 1) * P], sd_f[:, 0, T * P:(T + 1) * P], sd_f[:, 1, T * P:(T + 1) * P], start=True, stop=True)
                    pe.matmul(ps[64:P, 7, 256:320], sd_f[:, 0, SEQ:NT], sd_f[:, 1, SEQ:NT], start=True, stop=True).then_inc(S("sd_cb_full"), 1)

                def dta(T, h, n, rows=slice(0, P)):
                    return sd_tc[rows, 1, T, h:h + 1].broadcast_to([rows.stop - rows.start, n])

                sm = slice(64, P)

                def mix2(i):
                    for T, bank, read in ((0, 4, "sd_xt_read"), (1, 5, "sd_xs_read")):
                        pe.wait_ge(*past(read, i + 1))
                        for h in range(4):
                            mm = pe.matmul(ps[:, bank, h * P:(h + 1) * P], dta(T, h, P), upper[:], start=True, stop=True)
                        mm.then_inc(S(f"sd_seg{T}_full"), 1)
                    pe.wait_ge(*past("sd_bt_read", i + 1))
                    pe.wait_ge(*past("sd_cb_read", i + 1))
                    for h in range(4):
                        mm = pe.matmul(ps[:, 6, h * 64:(h + 1) * 64], dta(2, h, P, sm), s_causal[sm], start=True, stop=True)
                    mm.then_inc(S("sd_seg2_full"), 1)
                    for t in range(2):
                        c = 200 * t
                        for j in range(2):
                            out, h = ps[64 * j:64 * j + 64, 7], 2 * t + j
                            pe.matmul(out[:, c:c + P], dta(1, h, 64), upper[:], start=True, stop=True)
                            pe.matmul(out[:, c + P:c + 192], dta(2, h, 64, sm), s_causal[sm], start=True, stop=True)
                            mm = pe.matmul(out[:, c + 192:c + 200], dta(2, h, 64, sm), s_block[sm], start=True, stop=True)
                    mm.then_inc(S("sd_eo_full"), 1)

                def mix3(i):
                    pe.wait_ge(*past("sd_s0_in", i * 32 + 32))
                    for n, read in enumerate(("sd_seg0_ready", "sd_seg1_ready", "sd_seg2_ready", "sd_eo_read")):
                        pe.wait_ge(*past(read, i + 1))
                        for j in range(4):
                            b = 4 * (n % 2) + j
                            mm = pe.transpose(ps[:, 4 + n, j * P:(j + 1) * P], sd_s0[:, n // 2, b, :], ident[:])
                        mm.then_inc(S(f"sd_st{n}_full"), 1)
                    pe.wait_ge(*past("sd_xw_ready", i + 1))
                    pe.wait_ge(*past("sd_st0_read", i + 1))
                    pe.matmul(ps[:, 4, 0:256], sd_bt[:, 0, :], sd_xw[:, 0].rearrange("p h c -> p (h c)"), start=True, stop=True).then_inc(S("sd_s1_full"), 1)
                    for t in range(2):
                        pe.matmul(ps[:, 4, 256 + t * P:256 + (t + 1) * P], sd_xf[:, 2 * t:2 * t + 2, :].rearrange("p h c -> p (h c)"), sd_bt[:, 0, :], start=True, stop=False)
                        mm = pe.matmul(ps[:, 4, 256 + t * P:256 + (t + 1) * P], sd_xw[:, 1, 2 * t:2 * t + 2, :].rearrange("p h c -> p (h c)"), sd_bt[:, 1, :], start=False, stop=True)
                    mm.then_inc(S("sd_sf_full"), 1)
                    for t in range(2):
                        pe.wait_ge(*past(f"sd_st{1 + t}_read", i + 1))
                        if t == 0:
                            pe.wait_ge(*past("sd_m_ready", i + 1))
                            pe.wait_ge(*past("sd_st3_read", i + 1))
                            pe.wait_ge(*past("sd_s1_read", i + 1))
                        bank = 5 + t
                        pe.matmul(ps[:, bank, 320:448], sd_s1[:, t, :], sd_f[:, 1, P:2 * P], start=True, stop=True)
                        for j in range(2):
                            h = 2 * t + j
                            rows = slice(64 * j, 64 * j + 64)
                            for T in range(2):
                                pe.matmul(ps[rows, bank, T * P:(T + 1) * P], sd_xt[:, T, h, :], sd_e[:, T, h, :], start=True, stop=True)
                            pe.matmul(ps[rows, bank, 256:320], sd_xt[sm, 2, h, :], sd_e[sm, 2, h, 0:64], start=True, stop=True)
                        for b in range(NB):
                            c = SEQ + NL * b
                            mm = pe.matmul(ps[:, bank, 448 + NL * b:456 + NL * b], sd_st[:, t, b, :], sd_f[:, 1, c:c + NL], start=True, stop=True)
                        mm.then_inc(S(f"sd_y{t}_full"), 1)
                    for n, (bank, read) in enumerate(((7, None), (4, "sd_sf_read"), (5, "sd_y0_read"), (6, "sd_y1_read"))):
                        t, half = n // 2, n % 2
                        if read:
                            pe.wait_ge(*past(read, i + 1))
                        xw = sd_xw[sm, 2, 2 * t:2 * t + 2, :].rearrange("p h c -> p (h c)")
                        pe.matmul(ps[:, bank, :], xw, sd_bm[sm, 4 * half:4 * half + 4, :].rearrange("p b n -> p (b n)"), start=True, stop=True).then_inc(S(f"sd_sn{n}_full"), 1)

                def mix4(i):
                    pe.wait_ge(*past("sd_sn0_read", i + 1))
                    for t in range(2):
                        pe.wait_ge(*past("sd_ysq_ready", i * 2 + (t + 1)))
                        mm = pe.matmul(ps[:, 7, 0:NT], ones[:], sd_yo2[:, t, :], start=(t == 0), stop=(t == 1))
                    mm.then_inc(S("sd_ssq_full"), 1)
                    pe.wait_ge(*past("sd_sn1_read", i + 1))
                    for t in range(4):
                        mm = pe.transpose(ps[0:27, 4, t * P:(t + 1) * P], sd_pack[:, t, :], ident[:])
                    mm.then_inc(S("sd_so_full"), 1)

                def take_out(i):
                    pe.wait_ge(*past("sd_o_ready", i + 1))
                    pe.wait_ge(*past("sd_so_ready", i + 1))

                    def wait_read(t):
                        if t >= 4:
                            pe.wait_ge(*past("y_added", i * 8 + (8 * GROUPS + t - 3)))
                        elif t == 1:
                            pe.wait_ge(*past("sd_sn2_read", i + 1))
                            pe.wait_ge(*past("sd_sn3_read", i + 1))
                    project_rows(0, None, lambda t: 4 + t % 4, wait_read)
                    project_rows(1, None, lambda t: 4 + t % 4, wait_read)

                take_bc(0)
                take_x(0, 0)
                take_x(0, 1)
                take_z(0)
                with pe.Fori(1, GROUPS) as i:
                    units.enter(i, 1, 8)
                    take_bc(i)
                    mix1(i - 1)
                    take_x(i, 0)
                    mix2(i - 1)
                    take_x(i, 1)
                    mix3(i - 1)
                    mix4(i - 1)
                    take_z(i)
                    take_out(i - 1)
                    units.leave(GROUPS - 1)
                mix1(7)
                mix2(7)
                mix3(7)
                mix4(7)
                take_out(7)

            def hg():
                fresh.append(6 * KD)

                def turn_and_score(i, h):
                    if h == 0:
                        pe.wait_ge(*past("hg_K_ready", i + 1))
                    else:
                        pe.wait_ge(*past("hg_kt_read", i * 2 + 1))
                        pe.wait_ge(*past("hg_s1_read", i * 2 + 1))
                    for T in range(2):
                        pe.transpose(ps[:, 5, T * P:(T + 1) * P], hg_K[2 * h + T][:, 8, :], ident[:])
                    pe.transpose(ps[:, 5, 256:384], hg_k[:, h, NT - P:NT], ident[:]).then_inc(S("hg_kt_full"), 1)
                    if h == 1:
                        pe.wait_ge(*past("hg_att_ready", i * 2 + 1))
                        pe.wait_ge(*past("hg_sf_read", i * 2 + 1))
                    for T in range(2):
                        for c in range(8):
                            q = T * P + 16 * c
                            pe.matmul(ps[:, 4, q:q + 16], hg_K[2 * h + T][:, c, :], hg_q[:, h, q:q + 16], start=True, stop=True)
                    pe.matmul(ps[64:P, 4, 256:320], hg_ks[:, h, :], hg_q[:, h, SEQ:NT], start=True, stop=True).then_inc(S("hg_att_full"), 1)

                def states(i, h):
                    hv = slice(h * P, (h + 1) * P)
                    pe.wait_ge(*past("hg_kt_read", i * 2 + (h + 1)))
                    pe.matmul(ps[:, 5, 384:512], hg_kt[:, 0, :], hg_v[:, 0, hv], start=True, stop=True).then_inc(S("hg_s1_full"), 1)
                    pe.wait_ge(*past("hg_att_ready", i * 2 + (h + 1)))
                    pe.matmul(ps[:, 4, 384:512], hg_kt[:, 1, :], hg_v[:, 1, hv], start=True, stop=True).then_inc(S("hg_s2_full"), 1)
                    gain(i, h, 0)

                def gain(i, h, half):
                    if h == 0 and half == 0:
                        pe.wait_ge(*past("hg_vm_ready", i + 1))
                        if not (first(i) and i == 0):
                            pe.wait_ge(*past("hg_sn_read", i * 4))
                    else:
                        pe.wait_ge(*past("hg_sn_read", i * 4 + (2 * h + half)))
                    v = hg_vm[64:P, 4 * half:4 * half + 4, h * P:(h + 1) * P]
                    pe.matmul(ps[:, 7, :], hg_kt[64:P, 2, :], v, start=True, stop=True).then_inc(S("hg_sn_full"), 1)

                def outputs(i, h):
                    hv = slice(h * P, (h + 1) * P)
                    pe.wait_ge(*past("hg_s1_read", i * 2 + (h + 1)))
                    if h == 0:
                        pe.wait_ge(*past("hg_s0_in", i * 32 + 32))
                    if h == 1 or not (first(i) and i == 0):
                        pe.wait_ge(*past("hg_o_read", i * 2 + h))
                        pe.wait_ge(*past("hg_osq_ready", i * 2 + h))
                    o = lambda a, b: ps[:, 6, a:b]
                    pe.matmul(o(0, P), hg_v[:, 0, hv], hg_att[h][:, 0:P], start=True, stop=True)
                    pe.matmul(o(P, 2 * P), hg_v[:, 1, hv], hg_att[h][:, P:2 * P], start=True, stop=False)
                    pe.matmul(o(P, 2 * P), hg_s1[:, h, :], hg_x[:, h, 0:P], start=False, stop=True)
                    pe.matmul(o(2 * P, NT), hg_v[64:P, 2, hv], hg_att[h][64:P, 2 * P:NT], start=True, stop=False, skip_group_check=True)
                    for b in range(NB):
                        c = SEQ + NL * b
                        mm = pe.matmul(o(c, c + NL), hg_s0[:, h, b, :], hg_q[:, h, c:c + NL], start=False, stop=(b == NB - 1), skip_group_check=True)
                    mm.then_inc(S("hg_o_full"), 1)
                    gain(i, h, 1)

                def sums(i):
                    for h in range(2):
                        pe.wait_ge(*past("hg_osq_ready", i * 2 + (h + 1)))
                        if h == 0:
                            pe.wait_ge(*past("hg_sf_read", i * 2 + 2))
                        pe.matmul(ps[:, 4 + h, 0:NT], ones[:], hg_osq[:, h, :], start=True, stop=True).then_inc(S("hg_ssq_full"), 1)

                def body(i, mixed):
                    if not (first(i) and i == 0):
                        pe.wait_ge(*past("hg_f_read", i))
                    project(0, 0)
                    project(1, 1)
                    if mixed:
                        turn_and_score(i - 1, 0)
                        pe.wait_ge(*past("hg_v_read", i))
                    project(2, 0)
                    if mixed:
                        states(i - 1, 0)
                    project(3, 1)
                    if mixed:
                        rest(i - 1)
                    pe.wait_ge(*past("hg_g_read", i + 1))
                    project(0, 0)
                    project(1, 1)
                    if mixed:
                        sums(i - 1)
                    pe.wait_ge(*past("hg_q_read", i + 1))
                    halves(2)
                    for T in range(3):
                        t0 = (0, P, NT - P)[T]
                        out = ps[:, 2 + T // 2, 256 * (T % 2):256 * (T % 2) + 256]
                        for k in range(KD):
                            for n, (x, w) in enumerate(((Hh, wh), (Hh, wl), (Hl, wh))):
                                mm = pe.matmul(out, x[:, k, t0:t0 + P], w[:, :, k, :], start=(k == 0 and n == 0), stop=(k == KD - 1 and n == 2))
                    done(mm, 2)

                def rest(i):
                    outputs(i, 0)
                    turn_and_score(i, 1)
                    states(i, 1)
                    outputs(i, 1)

                body(0, False)
                with pe.Fori(1, GROUPS) as i:
                    units.enter(i, 1, 8)
                    body(i, True)
                    units.leave(GROUPS - 1)
                turn_and_score(7, 0)
                states(7, 0)
                rest(7)
                sums(7)
                pe.wait_ge(*past("hg_o_ready", GROUPS))
                for c in range(4):
                    if c >= 2:
                        pe.wait_ge(*past("y_added", 16 * GROUPS + 2 * c - 2))
                    for kc in range(2):
                        for j in range(2):
                            halves()
                            for k in range(8):
                                mm = three(ps[:, (2 * c + j) % 4, 0:NT], (j, k), Oh16[:, 8 * kc + k, :], Ol16[:, 8 * kc + k, :],
                                           kc == 0 and k == 0, kc == 1 and k == 7)
                            done(mm)

            def attention(L):
                hk = (2, 5, 8, 11)[L] * KD
                fresh.append(hk - KD)

                def memory(n):
                    if n >= 4:
                        pe.wait_ge(*past("at_kvt_ready", 16 * L + n - 3))
                    project(n % 4, n % 2, n=NMEM)

                def turn_memory(h):
                    pe.wait_ge(*past("at_kvt_ready", 16 * L + 2 * h + 2))
                    if 2 <= h < 6:
                        pe.wait_ge(*past("at_k_ready", XH * L + h - 1))
                    elif h >= 6:
                        pe.wait_ge(*past("at_v_ready", XH * L + h - 5))
                    for c in range(2):
                        t = 2 * (h % XH) + c
                        for a in range(2):
                            src = (at_kt if h < XH else at_vt)[:, t, a * P:(a + 1) * P]
                            mm = pe.transpose(ps[:, 4 + h % 2, 256 * a + P * c:256 * a + P * (c + 1)], src, ident[:])
                    mm.then_inc(S("at_turned_full"), 1)
                for n in range(16):
                    memory(n)
                    if n == 1:
                        sum_squares(2 + 4 * L, 6)
                    if n == 9:
                        sum_squares(3 + 4 * L, 7)
                    if n % 2 == 1 and n >= 3:
                        turn_memory((n - 3) // 2)
                turn_memory(7)
                fresh.append(hk)
                pe.wait_ge(*past("at_v_ready", XH * L + XH))
                for t in range(KD):
                    if t >= 4:
                        pe.wait_ge(*past("at_q_ready", KD * L + t - 3))
                    project(t % 4, t % 2)

                seen = 2 * NB * L
                pe.wait_ge(*past("at_q_ready", KD * L + KD))

                def turn_cache(n):
                    pe.wait_ge(*past(f"at_kb_in{n % 4}", 16 * (8 * L + n // 4 + 1)))
                    for g in range(2):
                        if n:
                            pe.wait_ge(*past(f"at_kbt{g}_ready", seen + n))
                        for j in range(4):
                            c = 4 * g + j
                            mm = pe.transpose(ps[:, 4 + g, j * P:(j + 1) * P], at_kb[n % 4][:, c * P:(c + 1) * P], ident[:])
                        mm.then_inc(S("at_kb_used" if g else "at_kbt_full"), 1)

                def cache_scores(n):
                    b, a = n // 2, n % 2
                    pe.wait_ge(*past("at_kbt0_ready", seen + n + 1))
                    pe.wait_ge(*past("at_kbt1_ready", seen + n + 1))
                    at = 256 * (b // 4) + P * a
                    rows = slice(32 * (b % 4), 32 * (b % 4) + 32)
                    for c in range(KD):
                        mm = pe.matmul(ps[rows, 7, at:at + P], at_qz[:, b, c, :], at_kbt[:, n % 2, c, :], start=(c == 0), stop=(c == KD - 1))
                    mm.then_inc(S("at_cs_full"), 1)

                def prompt_scores(T):
                    for h in range(XH):
                        for c in range(2):
                            mm = pe.matmul(ps[:, 2 * T + h // 2, 256 * (h % 2):256 * (h % 2) + 256], at_q[:, 2 * h + c, T * P:(T + 1) * P],
                                           at_kt[:, 2 * h + c, :], start=(c == 0), stop=(c == 1))
                    mm.then_inc(S("at_s_full"), 1)

                def prompt_turn(T):
                    pe.wait_ge(*past("at_pp_ready", 2 * L + T + 1))
                    for g in range(2):
                        if T == 1:
                            pe.wait_ge(*past("at_ppt_read", 4 * L + g + 1))
                        for h in range(2):
                            for a in range(2):
                                mm = pe.transpose(ps[:, 4 + g, (2 * h + a) * P:(2 * h + a + 1) * P], at_pp[:, 2 * g + h, a * P:(a + 1) * P], ident[:])
                        mm.then_inc(S("at_ppt_full"), 1)

                turn_cache(0)
                pe.wait_ge(*past("at_qz_ready", L + 1))
                for n in range(1, 16):
                    turn_cache(n)
                    cache_scores(n - 1)
                cache_scores(15)
                prompt_scores(0)
                prompt_scores(1)
                pe.wait_ge(*past(f"at_kbt0_ready", seen + 16))
                prompt_turn(0)
                prompt_turn(1)
                pe.wait_ge(*past("at_p_ready", L + 1))
                for a in range(2):
                    for hb in range(2):
                        mm = pe.transpose(ps[:, 6, a * 256 + hb * P:a * 256 + (hb + 1) * P], at_p[:, hb, a * P:(a + 1) * P], ident[:])
                mm.then_inc(S("at_pt_full"), 1)
                pe.wait_ge(*past("at_v_ready", XH * L + XH))
                pe.wait_ge(*past("at_ppt_read", 4 * L + 4))
                for c in range(KD):
                    for a in range(2):
                        mm = pe.matmul(ps[:, c // 2, 256 * (c % 2):256 * (c % 2) + 256], at_v[:, a, c * P:(c + 1) * P], at_ppt[:, c // 2, a, :],
                                       start=(a == 0), stop=(a == 1))
                mm.then_inc(S("at_o_full"), 1)
                pe.wait_ge(*past("at_pt_ready", L + 1))
                for n in range(16):
                    b, a = n // 2, n % 2
                    pe.wait_ge(*past(f"at_kb_in{n % 4}", 16 * (8 * L + 4 + n // 4 + 1)))
                    rows, at = slice(32 * (b % 4), 32 * (b % 4) + 32), 256 * (b // 4)
                    for h in range(XH):
                        mm = pe.matmul(ps[rows, 7, at:at + 256], at_ptz[:, a, b, h, :], at_kb[n % 4][:, h * 256:(h + 1) * 256],
                                       start=(a == 0 and h == 0), stop=(a == 1 and h == XH - 1))
                    mm.then_inc(S("at_kb_used"), 1)
                pe.wait_ge(*past("at_so_ready", L + 1))
                for hb in range(2):
                    for c in range(2):
                        mm = pe.transpose(ps[:, 6, 256 * hb + P * c:256 * hb + P * (c + 1)], at_so[:, hb, c * P:(c + 1) * P], ident[:])
                mm.then_inc(S("at_so_full"), 1)
                pe.wait_ge(*past("at_o_ready", L + 1))
                for t in range(KD):
                    if t >= 4:
                        pe.wait_ge(*past("at_y_ready", KD * L + t - 3))
                    project(t % 4, t % 2, Oh, Ol)
                sum_squares(4 + 4 * L, 6)
                if L < DEPTH - 1:
                    sum_squares(5 + 4 * L, 7)

            rg(0)
            attention(0)
            ssd()
            attention(1)
            hg()
            attention(2)
            rg(1)
            attention(3)
            for k in range(KD):
                pe.wait_ge(*past("x_ready", 2 * DEPTH * KD + k + 1))
                for a in range(3):
                    t0 = (0, P, NT - P)[a]
                    mm = pe.transpose(ps[:, k, a * P:(a + 1) * P], X[:, k, t0:t0 + P], ident[:])
                mm.then_inc(S("yt_full"), 1)

        @block.gpsimd
        def _(pool):
            steps = Chain(pool, S("pool_steps"))

            def mask(out, pattern, base, mult, op, src=None):
                steps.did(pool.affine_select(out=out, in_=out if src is None else src, pattern=pattern, compare_op=op,
                                             fill=0.0, base=base, channel_multiplier=mult))
                steps.sync()

            steps.did(pool.memset(eps_c, EPS))
            steps.did(pool.memset(tiny_c, TINY))
            pool.memset(raw[:, 2, 4:8, :], 0.0).then_inc(S("raw_clear"), 1)
            for t in (ones, ident, upper, later, s_causal, s_later, s_block, dmask):
                steps.did(pool.memset(t[:], 1.0))
            steps.did(pool.memset(restart[:], 1.0))
            steps.sync()
            mask(ident[:], [[-1, P]], 0, 1, ALU.is_equal)
            mask(upper[:], [[1, P]], 0, -1, ALU.is_ge)
            mask(later[:], [[-1, P]], -1, 1, ALU.is_ge)
            seq = [[-NL, NB], [0, NL]]
            v = s_causal.rearrange("p (b t) -> p b t", b=NB)
            mask(v, seq, -64, 1, ALU.is_ge)
            mask(v, [[NL, NB], [1, NL]], 64, -1, ALU.is_ge)
            v = s_later.rearrange("p (b t) -> p b t", b=NB)
            mask(v, [[-NL, NB], [-1, NL]], -65, 1, ALU.is_ge)
            mask(v, [[NL, NB], [0, NL]], 64 + NL - 1, -1, ALU.is_ge)
            mask(s_block[:], [[-NL, NB]], -64, 1, ALU.is_ge)
            mask(s_block[:], [[NL, NB]], 64 + NL - 1, -1, ALU.is_ge)
            mask(dmask.rearrange("p (a b) -> p a b", a=9), [[1, 9], [-1, 8]], 0, 0, ALU.is_ge)
            v = restart[:, 0:SEQ].rearrange("p (c t) -> p c t", t=16)
            steps.did(pool.memset(v[:, :, 0:1], 0.0))
            v = restart[:, SEQ:NT].rearrange("p (c t) -> p c t", t=8)
            steps.did(pool.memset(v[:, :, 0:1], 0.0))
            steps.sync()
            pool.memset(smallc[:, 3:4], 0.0).then_inc(S("consts"), 1)

            def low(n, slot, half, peeled):
                pool.wait_ge(hi_ready, n + 1)
                if not peeled:
                    pool.wait_ge(used, n - 1)
                src = raw[:, slot, :, half * P:(half + 1) * P]
                pool.tensor_tensor(wl[:, half], src, wh[:, half].bitcast(F32), ALU.subtract).then_inc(lo_ready, 1)

            for n in range(8):
                low(n, n // 2, n % 2, n < 2)
            with pool.Fori(1, N_UNITS // 8) as r:
                for n in range(8):
                    low(r * 8 + n, n // 2, n % 2, False)

        @block.scalar
        def _(act):
            steps = Chain(act, S("act_steps"))
            nx = Count()

            def split():
                n = nx.n
                slot, half = n // 2 % SLOTS, n % 2
                if nx.i is None:
                    act.wait_ge(landed[slot], 64 * (n // 8 + 1))
                else:
                    act.wait_ge(landed[slot], (nx.i + (n // 8 + 1 - nx.i0)) * 64)
                if n >= 2:
                    act.wait_ge(used, nx.at(-1))
                act.activation(wh[:, half], raw[:, slot, :, half * P:(half + 1) * P], ACT.Copy).then_inc(hi_ready, 1)
                nx.n += 1

            def upto(n):
                while nx.n < min(n, N_UNITS):
                    split()

            def squares(n, src, k0=0):
                for k in range(KD):
                    src(k)
                    act.activation(SQ[:, k, 0:sq_width[0]], sq_src[0][:, k], ACT.Square).then_inc(S("sq_ready"), 1)

            sq_width, sq_src = [NT], [None]

            def square(src, wait, width=NT):
                sq_width[0], sq_src[0] = width, src
                squares(0, wait)

            def root(n, bank, width=NT):
                act.wait_ge(*past("ssq_full", n + 1))
                act.wait_ge(*past("rs_used", n)) if n else None
                steps.did(act.activation(rs[:, 0:width], ps[:, bank, 0:width], ACT.Ln, bias=eps_c, scale=1.0 / D))
                steps.sync()
                act.activation(rs[:, 0:width], rs[:, 0:width], ACT.Exp, scale=-0.5).then_inc(S("rs_ready"), 1)

            def high(n):
                for k in range(KD):
                    act.wait_ge(*past("h_full", KD * n + k + 1))
                    w = NMEM if n % 3 == 1 else NT
                    src = memh if n % 3 == 1 else Y
                    act.activation(Hh[:, k, 0:w], src[:, k, 0:w], ACT.Copy).then_inc(S("h_high"), 1)

            act.preload_act_table_set(EXP_SET)
            act.wait_ge(*past("consts", 1))
            upto(2)
            square(memn, lambda k: act.wait_ge(*past("mem_ready", k + 1)), NMEM)
            root(0, 6, NMEM)
            for k in range(KD):
                act.wait_ge(*past("x_ready", k + 1))
                act.wait_ge(*past("ssq_full", 1))
                act.activation(SQ[:, k, :], X[:, k], ACT.Square).then_inc(S("sq_ready"), 1)
            root(1, 7)
            act.wait_ge(*past("lam_abs", 1))
            act.activation(lam_e, lam_e, ACT.Exp, scale=-1.0).then_inc(S("lam_exp"), 1)
            act.wait_ge(*past("lb_diff", 1))
            act.activation(lb_e, lb_e, ACT.Exp).then_inc(S("lb_exp"), 1)
            high(0)

            def rg(l):
                i0 = 8 * l

                def at(i, what):
                    return after("rg", i, i0, what)

                def enter(i):
                    n0 = i if first(i) else i0 + 1
                    upto(at(n0, "u") + 1)
                    act.wait_ge(*past("rg_ht_full", i + 1))
                    if not (first(i) and i == 0):
                        act.wait_ge(*past("rg_in_read", i))
                    steps.did(act.activation(rg_in[:, :, 3:SC], ps[:, 0:2, 0:SEQ], ACT.Copy))
                    act.activation(samples(rg_in, SC)[:, :, :, 3:SEG], ps[:, 0:2, SEQ:NT].rearrange("p t (b s) -> p t b s", b=NB), ACT.Copy).then_inc(S("rg_u_in"), 1)
                    upto(at(n0, "g") + 1)
                    act.wait_ge(used, at(i, "g"))
                    if not (first(i) and i == 0):
                        act.wait_ge(*past("rg_o_done", i))
                    act.activation(rg_gate, ps[:, 2:4, 0:NT], ACT.Sigmoid).then_inc(S("rg_gate_sig"), 1)
                    act.wait_ge(*past("rg_conv_done", i + 1))
                    act.activation(ug[:, 0, :, 0:CV], rg_u[:, :, 0:CV], ACT.Copy).then_inc(S("rg_u_high"), 1)

                def gates(i, last):
                    n0 = i if first(i) else i0 + 1
                    r0 = at(n0, "r")
                    upto(r0 + 1)
                    act.wait_ge(used, at(i, "r") - 1)
                    for j in range(2):
                        steps.did(act.activation(rg_r[:, j, 0:CV], ps[:, 4 + j, 0:CV], ACT.Sigmoid, bias=rg_cur[:, 5, j:j + 1]))
                    act.wait_ge(used, at(i, "r"))
                    upto(r0 + 2)
                    for j in range(2):
                        ins = act.activation(rg_i[:, j, 0:CV], ps[:, 6 + j, 0:CV], ACT.Sigmoid, bias=rg_cur[:, 6, j:j + 1])
                        if j:
                            ins.then_inc(S("rg_ri_read"), 1)
                        else:
                            steps.did(ins)
                    steps.sync()
                    for j in range(2):
                        steps.did(act.activation(rg_t[:, j, 0:CV], rg_r[:, j, 0:CV], ACT.Tanh, scale=rg_cur[:, 8, j:j + 1]))
                    act.preload_act_table_set(EXP_SET)
                    if not last:
                        upto(r0 + 3)
                    for j in range(2):
                        steps.did(act.activation(rg_a[:, j, 0:CV], rg_r[:, j, 0:CV], ACT.Exp, scale=rg_cur[:, 7, j:j + 1]))
                    steps.sync()
                    act.activation(rg_r[:, :, 0:CV], rg_a[:, :, 0:CV], ACT.Square).then_inc(S("rg_a_ready"), 1)
                    if not last:
                        upto(r0 + 4)
                    act.wait_ge(*past("rg_v_ready", i + 1))
                    steps.did(act.activation(rg_t[:, :, 0:CV], rg_t[:, :, 0:CV], ACT.Ln, bias=tiny_c))
                    steps.sync()
                    act.activation(rg_t[:, :, 0:CV], rg_t[:, :, 0:CV], ACT.Exp, scale=0.5).then_inc(S("rg_root"), 1)
                    act.preload_act_table_set(SIG_SET)
                    if not last:
                        upto(r0 + 5)
                    act.wait_ge(*past("rg_o_done", i + 1))
                    if not (first(i) and i == i0):
                        act.wait_ge(used, at(i, "out"))
                    act.activation(Oh[:, 0:2, :], rg_o, ACT.Copy).then_inc(S("rg_o_high"), 1)
                    upto(r0 + (2 if last else 6))

                act.preload_act_table_set(SIG_SET)
                enter(i0)
                gates(i0, False)
                with act.Fori(i0 + 1, i0 + 7) as i:
                    nx.enter(i, i0 + 1, 8)
                    steps.count.enter(i, i0 + 1, RG_STEPS)
                    enter(i)
                    gates(i, False)
                    nx.leave(6)
                    steps.count.leave(6)
                enter(i0 + 7)
                gates(i0 + 7, True)

            def ssd():
                at = lambda i, what: after("ssd", i, 0, what)
                act.wait_ge(*past("in_wdt", 16))
                act.activation(wdth[:], wdt[:], ACT.Copy).then_inc(S("sd_wdt_high"), 1)
                act.wait_ge(*past("sd_dt_abs", 1))
                act.activation(sd_tw[:, 1], sd_tw[:, 1], ACT.Exp, scale=-1.0).then_inc(S("sd_dt_exp"), 1)
                act.wait_ge(*past("in_head", 64))
                act.activation(alog, alog, ACT.Exp).then_inc(S("sd_a"), 1)
                act.wait_ge(*past("sd_sums_full", 1))
                w = sd_ta.rearrange("p c t h -> p c (t h)")
                steps.did(act.activation(w[:, 2, 0:64], ps[:, 1, 0:64], ACT.Copy))
                steps.did(act.activation(w[64:P, 2, 64:96], ps[64:P, 1, 64:96], ACT.Copy))
                steps.did(act.activation(w[:, 3, 0:64], ps[:, 1, 96:160], ACT.Exp))
                steps.did(act.activation(w[64:P, 3, 64:96], ps[64:P, 1, 160:192], ACT.Exp))
                act.activation(w[:, 4, 0:32], ps[:, 1, 192:224], ACT.Exp).then_inc(S("sd_sums_read"), 1)

                def take_in(i):
                    act.wait_ge(used, at(i, "x"))
                    if not (first(i) and i == 0):
                        act.wait_ge(*past("sd_in_read", i))
                    steps.did(act.activation(sd_in[:, :, 3:SC], ps[:, 0:4, 0:SEQ], ACT.Copy))
                    act.activation(samples(sd_in, SC)[:, :, :, 3:SEG], ps[:, 0:4, SEQ:NT].rearrange("p t (b s) -> p t b s", b=NB), ACT.Copy).then_inc(S("sd_in_ready"), 1)

                def enter(i):
                    n0 = i if first(i) else 1
                    upto(at(n0, "x") + 1)
                    if first(i) and i == 0:
                        take_in(0)
                    upto(at(n0, "z") + 1)
                    act.preload_act_table_set(SIG_SET)
                    act.wait_ge(used, at(i, "z"))
                    act.activation(sd_z, ps[:, 0:2, 0:NT], ACT.Sigmoid).then_inc(S("sd_z_sig"), 1)
                    if not (first(i) and i == 0):
                        upto(at(n0, "out"))
                    act.wait_ge(*past("sd_conv_done", i + 1))
                    steps.did(act.activation(sd_sig[:, :, 0:SEQ], sd_c[:, :, 0:SEQ], ACT.Sigmoid))
                    act.activation(sd_sig[:, :, SEQ:NT].rearrange("p t (b s) -> p t b s", b=NB), samples(sd_c, SC)[:, :, :, 0:NL], ACT.Sigmoid).then_inc(S("sd_sig_ready"), 1)
                    act.preload_act_table_set(EXP_SET)

                def mix(i, last):
                    n0 = i if first(i) else 1
                    if last:
                        upto(at(n0, "out") + 2)
                        left = [0] * 5
                    else:
                        base = at(n0, "z") if first(i) else at(n0, "out")
                        left = [base + 2, base + 2, base + 3, base + 4, base + 5]
                    upto(left[0])
                    act.wait_ge(*past("sd_bt_full", i + 1))
                    act.activation(sd_bt[:, 0:2, :], ps[:, 6, 0:256].rearrange("p (a n) -> p a n", a=2), ACT.Copy).then_inc(S("sd_bt_read"), 1)
                    upto(left[2])
                    for T in range(3):
                        act.wait_ge(*past(f"sd_seg{T}_ready", i + 1))
                        rows, w = (slice(0, P), P) if T < 2 else (slice(64, P), 64)
                        ins = act.activation(sd_e[rows, T, :, 0:w], sd_e[rows, T, :, 0:w], ACT.Exp)
                        ins.then_inc(S(f"sd_exp{T}"), 1)
                    act.wait_ge(*past("sd_eo_full", i + 1))
                    act.activation(sd_eo, ps[:, 7, 0:400].rearrange("p (t c) -> p t c", t=2), ACT.Exp).then_inc(S("sd_eo_read"), 1)
                    upto(left[3])
                    for n in range(4):
                        act.wait_ge(*past(f"sd_st{n}_full", i + 1))
                        act.activation(sd_st[:, n // 2, 4 * (n % 2):4 * (n % 2) + 4, :], ps[:, 4 + n, :].rearrange("p (b c) -> p b c", b=4), ACT.Copy).then_inc(S(f"sd_st{n}_read"), 1)
                    act.wait_ge(*past("sd_sf_full", i + 1))
                    act.activation(sd_s1, ps[:, 4, 0:256].rearrange("p (t c) -> p t c", t=2), ACT.Copy).then_inc(S("sd_s1_read"), 1)
                    act.wait_ge(*past("sd_sf_full", i + 1))
                    if not (first(i) and i == 0):
                        act.wait_ge(*past("sd_stored", i * 48))
                    act.activation(sd_sf, ps[:, 4, 256:512].rearrange("p (t c) -> p t c", t=2), ACT.Copy).then_inc(S("sd_sf_read"), 1)
                    if not last:
                        take_in(i + 1)
                    upto(left[4])
                    for t in range(2):
                        act.wait_ge(*past("sd_yz_ready", i * 2 + (t + 1)))
                        act.activation(sd_yo2[:, t, :], sd_y[:, t, :], ACT.Square).then_inc(S("sd_ysq_ready"), 1)
                    act.wait_ge(*past("sd_ssq_full", i + 1))
                    steps.did(act.activation(sd_rs, ps[:, 7, 0:NT], ACT.Ln, bias=eps_c, scale=1.0 / 256))
                    steps.sync()
                    act.activation(sd_rs, sd_rs, ACT.Exp, scale=-0.5).then_inc(S("sd_rs_ready"), 1)
                    act.wait_ge(*past("sd_y_done", i + 1))
                    if not (first(i) and i == 0):
                        act.wait_ge(used, at(i, "out"))
                    act.activation(Oh[:, 0:2, :], sd_y, ACT.Copy).then_inc(S("sd_o_high"), 1)

                enter(0)
                mix(0, False)
                with act.Fori(1, 7) as i:
                    nx.enter(i, 1, 8)
                    steps.count.enter(i, 1, SSD_STEPS)
                    enter(i)
                    mix(i, False)
                    nx.leave(6)
                    steps.count.leave(6)
                enter(7)
                mix(7, True)

            def hg():
                at = lambda i, what: after("hg", i, 0, what)

                def mix(i, h):
                    act.wait_ge(*past("hg_s1_full", i * 2 + (h + 1)))
                    act.activation(hg_s1[:, h, :], ps[:, 5, 384:512], ACT.Copy).then_inc(S("hg_s1_read"), 1)

                def square_out(i, h):
                    act.wait_ge(*past("hg_o_full", i * 2 + (h + 1)))
                    act.activation(hg_osq[:, h, :], ps[:, 6, 0:NT], ACT.Square).then_inc(S("hg_osq_ready"), 1)

                def sums(i):
                    for h in range(2):
                        act.wait_ge(*past("hg_ssq_full", i * 2 + (h + 1)))
                        steps.did(act.activation(hg_rs[:, h, :], ps[:, 4 + h, 0:NT], ACT.Ln, bias=eps_c, scale=1.0 / P))
                    steps.sync()
                    act.activation(hg_rs, hg_rs, ACT.Exp, scale=-0.5).then_inc(S("hg_rs_ready"), 1)

                def body(i, mixed):
                    b = MIX_AT[2] + 8 * (1 if not first(i) else i)
                    upto(b + 3)
                    if mixed:
                        mix(i - 1, 0)
                    upto(b + 5)
                    if mixed:
                        square_out(i - 1, 0)
                        mix(i - 1, 1)
                        square_out(i - 1, 1)
                    act.wait_ge(used, at(i, "g"))
                    if mixed:
                        act.wait_ge(*past("hg_o_read", i * 2))
                    act.activation(hg_g, ps[:, 0:2, 0:NT], ACT.Sigmoid).then_inc(S("hg_g_sig"), 1)
                    act.wait_ge(used, at(i, "q"))
                    if mixed:
                        act.wait_ge(*past("hg_sn_read", i * 4))
                    act.activation(hg_q, ps[:, 2:4, 0:NT], ACT.Sigmoid).then_inc(S("hg_q_sig"), 1)
                    upto(b + 7)
                    act.wait_ge(used, at(i, "f"))
                    steps.did(act.activation(hg_f, ps[:, 0:2, 0:NT], ACT.Sigmoid))
                    act.activation(hg_k, ps[:, 0:2, 0:NT], ACT.Sigmoid, scale=-1.0).then_inc(S("hg_f_read"), 1)
                    act.preload_act_table_set(EXP_SET)
                    upto(b + 8)
                    if mixed:
                        sums(i - 1)
                    act.wait_ge(*past("hg_forget", i + 1))
                    act.activation(hg_f, hg_f, ACT.Ln).then_inc(S("hg_logf"), 1)
                    act.wait_ge(*past("hg_G_ready", i + 1))
                    steps.did(act.activation(hg_D, hg_D, ACT.Exp))
                    steps.did(act.activation(hg_eA, hg_A, ACT.Exp))
                    steps.did(act.activation(hg_eg, hg_gt[:, :, 16:24], ACT.Exp))
                    act.activation(hg_en, hg_gt[:, :, 16:24], ACT.Exp, scale=-1.0).then_inc(S("hg_D_ready"), 1)
                    steps.did(act.activation(hg_x, hg_x, ACT.Exp))
                    act.activation(hg_G, hg_G, ACT.Exp).then_inc(S("hg_exps"), 1)
                    upto(b + 9)
                    act.wait_ge(used, at(i, "v"))
                    steps.did(act.activation(hg_v[:, 0:2, :], ps[:, 2, :].rearrange("p (a n) -> p a n", a=2), ACT.Copy))
                    act.activation(hg_v[:, 2, :], ps[:, 3, 0:256], ACT.Copy).then_inc(S("hg_v_read"), 1)
                    act.preload_act_table_set(SIG_SET)
                    upto(b + 10)

                body(0, False)
                with act.Fori(1, GROUPS) as i:
                    nx.enter(i, 1, 8)
                    steps.count.enter(i, 1, HG_STEPS)
                    body(i, True)
                    nx.leave(GROUPS - 1)
                    steps.count.leave(GROUPS - 1)
                mix(7, 0)
                square_out(7, 0)
                mix(7, 1)
                square_out(7, 1)
                act.preload_act_table_set(EXP_SET)
                sums(7)
                for n in range(OUT_AT, OUT_AT + OUT_UNITS):
                    upto(n + 2)

            def attention(L):
                a0 = ATT_AT[L]
                act.preload_act_table_set(EXP_SET)
                high(3 * L + 1)

                def take(n):
                    act.wait_ge(used, a0 + n + 1)
                    out = at_kt[:, n, :] if n < KD else at_vt[:, n - KD, 0:NMEM]
                    act.activation(out, ps[:, n % 4, 0:NMEM], ACT.Copy).then_inc(S("at_kvt_ready"), 1)

                def y_squares():
                    for k in range(KD):
                        act.wait_ge(*past("y_added", Y_DONE[L]))
                        act.activation(SQ[:, k, :], Y[:, k], ACT.Square).then_inc(S("sq_ready"), 1)

                def x_squares(n):
                    for k in range(KD):
                        act.wait_ge(*past("x_ready", KD * (n + 1) + k + 1))
                        if k == 0:
                            act.wait_ge(*past("ssq_full", 3 + 2 * n))
                        act.activation(SQ[:, k, :], X[:, k], ACT.Square).then_inc(S("sq_ready"), 1)

                upto(a0 + 2)
                y_squares()
                for n in range(16):
                    upto(a0 + n + 2)
                    take(n)
                    if n == 1:
                        upto(a0 + n + 3)
                        root(2 + 4 * L, 6)
                    if n == 7:
                        upto(a0 + n + 3)
                        x_squares(2 * L)
                    if n == 11:
                        upto(a0 + n + 3)
                        root(3 + 4 * L, 7)
                high(3 * L + 2)
                for t in range(KD):
                    upto(a0 + 16 + t + 2)
                seen = 16 * L

                for n in range(16):
                    act.wait_ge(*past("at_kbt_full", seen + n + 1))
                    if n >= 2:
                        act.wait_ge(*past("at_cs_full", seen + n - 1))
                    act.activation(at_kbt[:, n % 2, 0:4, :], ps[:, 4, :].rearrange("p (c m) -> p c m", c=4), ACT.Copy).then_inc(S("at_kbt0_ready"), 1)
                for T in range(2):
                    act.wait_ge(*past("at_m_ready", 2 * L + T + 1))
                    for h in range(XH):
                        ins = act.activation(at_pp[:, h, :], ps[:, 2 * T + h // 2, 256 * (h % 2):256 * (h % 2) + 256], ACT.Exp,
                                             bias=at_m[:, 1 + T, h:h + 1], accum_out=at_m[:, 3 + T, h:h + 1])
                        if h < XH - 1:
                            steps.did(ins)
                    ins.then_inc(S("at_e_ready"), 1)
                    if T == 0:
                        act.wait_ge(*past("at_ppt_full", 4 * L + 2))
                act.wait_ge(*past("at_ms_ready", L + 1))
                for hb in range(2):
                    ins = act.activation(at_p[:, hb, :], ps[:, 7, 256 * hb:256 * hb + 256], ACT.Exp,
                                         bias=at_m[:, 5, hb:hb + 1], accum_out=at_m[:, 6, hb:hb + 1])
                    if hb == 0:
                        steps.did(ins)
                ins.then_inc(S("at_es_ready"), 1)
                act.wait_ge(*past("at_kb_used", 32 * L + 32))
                act.activation(at_so, ps[:, 7, :].rearrange("p (a c) -> p a c", a=2), ACT.Copy).then_inc(S("at_so_ready"), 1)
                act.wait_ge(*past("at_o_whole", L + 1))
                act.activation(Oh[:, 0:KD, :], at_q, ACT.Copy).then_inc(S("at_o_high"), 1)
                for t in range(KD):
                    upto(a0 + 24 + t + 2)
                    act.wait_ge(used, a0 + 24 + t + 1)
                    act.activation(Y[:, t], ps[:, t % 4, 0:NT], ACT.Copy).then_inc(S("at_y_ready"), 1)
                    for k in [t - 1] * (t > 0) + [t] * (t == KD - 1):
                        act.wait_ge(*past("at_y_ready", KD * L + k + 1))
                        act.activation(SQ[:, k, :], Y[:, k], ACT.Square).then_inc(S("sq_ready"), 1)
                root(4 + 4 * L, 6)
                if L < DEPTH - 1:
                    x_squares(2 * L + 1)
                    root(5 + 4 * L, 7)
                    high(3 * L + 3)

            rg(0)
            attention(0)
            ssd()
            attention(1)
            hg()
            attention(2)
            rg(1)
            attention(3)

        @block.vector
        def _(dve):
            steps = Chain(dve, S("dve_steps"))
            did, sync = steps.did, steps.sync
            wait = lambda name, n: dve.wait_ge(*past(name, n))
            tt, ts, stt = dve.tensor_tensor, dve.tensor_scalar, dve.scalar_tensor_tensor
            MUL, ADD, SUB, MAX, MIN = ALU.mult, ALU.add, ALU.subtract, ALU.max, ALU.min

            def copy(out, src):
                return ts(out, src, 1.0, None, MUL)

            def apart(v):
                return samples(v, SC)[:, :, :, 0:NL]

            def by_seq(v):
                return v[:, :, SEQ:NT].rearrange("p t (b s) -> p t b s", b=NB)

            def log1p(e, z, s, out):
                did(ts(z, e, 2.0, None, ADD))
                sync()
                did(dve.reciprocal(z, z))
                sync()
                did(tt(z, z, e, MUL))
                sync()
                did(tt(s, z, z, MUL))
                sync()
                did(ts(out, s, 1.0 / 17, 1.0 / 15, MUL, ADD))
                for d in (13, 11, 9, 7, 5, 3, 1):
                    sync()
                    did(tt(out, out, s, MUL))
                    sync()
                    did(ts(out, out, 1.0 / d, None, ADD))
                sync()
                did(stt(out, out, 2.0, z, MUL, MUL))
                sync()

            def normal(n, root, src, g, dst=None, width=NT):
                dst = Y if dst is None else dst
                for k in range(KD):
                    if root is None:
                        ins = ts(dst[:, k, 0:width], src[:, k, 0:width], g(k), None, MUL)
                    else:
                        if k == 0:
                            wait("rs_ready", root + 1)
                        ins = stt(dst[:, k, 0:width], src[:, k, 0:width], g(k), rs[:, 0:width], MUL, MUL)
                    ins.then_inc(S("h_full"), 1)
                if root is not None:
                    wait("h_full", KD * n + KD)
                    dve.sem_inc(S("rs_used"), 1)
                for k in range(KD):
                    wait("h_high", KD * n + k + 1)
                    tt(Hl[:, k, 0:width], dst[:, k, 0:width], Hh[:, k, 0:width].bitcast(F32), SUB).then_inc(S("h_ready"), 1)

            def residual(root, g):
                wait("rs_ready", root + 1)
                for k in range(KD + 1):
                    if k < KD:
                        did(stt(Y[:, k], Y[:, k], g(k), rs[:], MUL, MUL))
                    if k > 0:
                        dve.wait_ge(steps.sem, steps.count.at(-1 if k < KD else 0))
                        tt(X[:, k - 1], X[:, k - 1], Y[:, k - 1], ADD).then_inc(S("x_ready"), 1)
                dve.sem_inc(S("rs_used"), 1)

            def gain(L, j):
                return lambda k: par[:, 0, (L * 4 + j) * 8 + k:(L * 4 + j) * 8 + k + 1]

            wait("pro_full", 1)
            copy(par[:, 0:4, :], ps[:, 0, :].rearrange("p (a n) -> p a n", a=4)).then_inc(S("par_read"), 1)
            wait("pro_full", 2)
            did(copy(par[:, 4, :], ps[:, 1, 0:P]))
            copy(par[:, 5, 0:32], ps[:, 1, P:P + 32]).then_inc(S("par_read"), 1)
            for k in range(KD):
                bank = (2 + k) % 8
                wait("pro_full", 3 + k)
                did(copy(X[:, k, 0:SEQ], ps[:, bank, 0:SEQ]))
                copy(X[:, k, SEQ:NT], ps[:, bank, 320:384]).then_inc(S("x_ready"), 1)
            for k in range(KD):
                wait("pro_full", 11 + k)
                copy(memn[:, k], ps[:, (2 + k) % 8, 0:NMEM]).then_inc(S("mem_ready"), 1)
            sync()
            wait("par_read", 2)
            wait("consts", 1)
            for j in range(3):
                did(copy(rgc[:, j], par[:, 2, 32 * j:32 * j + 32].rearrange("p (l t) -> p l t", l=2)))
            lam = par[:, 2, 96:128]
            stt(lam_e, lam, -1.0, lam, MUL, MAX).then_inc(S("lam_abs"), 1)
            v = par[:, 4, 64:128].rearrange("p (l t) -> p l t", l=4)
            e = lb_e.rearrange("p (l t) -> p l t", l=4)
            did(tt(lb, v[:, 0], v[:, 1], MAX))
            sync()
            did(tt(lb, lb, v[:, 2], MAX))
            sync()
            did(tt(lb, lb, v[:, 3], MAX))
            sync()
            tt(e, v, lb.unsqueeze(1).broadcast_to([P, 4, 16]), SUB).then_inc(S("lb_diff"), 1)
            wait("rs_ready", 1)
            for k in range(KD):
                did(tt(memn[:, k], memn[:, k], rs[:, 0:NMEM], MUL))
            sync()
            dve.sem_inc(S("rs_used"), 1)
            normal(0, 1, X, gain(0, 0))
            wait("lam_exp", 1)
            c3, c4 = (rgc[:, j].rearrange("p l t -> p (l t)") for j in (3, 4))
            log1p(lam_e, tmp32[:, 0:32], tmp32[:, 32:64], c4)
            did(ts(c3, lam, -1.0, 0.0, MUL, MAX))
            sync()
            did(tt(c4, c4, c3, ADD))
            sync()
            did(ts(c3, c4, -8.0, None, MUL))
            sync()
            did(ts(c4, c3, -1.0, None, MUL))
            wait("lb_exp", 1)
            did(tt(lb, e[:, 1], e[:, 2], ADD))
            did(tt(oml, e[:, 0], e[:, 3], ADD))
            sync()
            did(tt(tmp32[:, 0:16], lb, oml, ADD))
            sync()
            did(dve.reciprocal(tmp32[:, 0:16], tmp32[:, 0:16]))
            sync()
            did(tt(lb, lb, tmp32[:, 0:16], MUL))
            did(tt(oml, oml, tmp32[:, 0:16], MUL))
            sync()

            def add_out(n, out_count):
                for s in range(8):
                    h, q = s // 4, s % 4
                    if q < 3:
                        wait("out_full", out_count(3 * h + q + 1))
                    else:
                        dve.wait_ge(used, n - 1 + h)
                    t = 2 * q + h
                    tt(Y[:, t], Y[:, t], ps[:, 4 + q, 0:NT], ADD).then_inc(S("y_added"), 1)

            def rg(l):
                i0 = 8 * l
                outs = 0 if l == 0 else 2 * 6 * GROUPS

                def finish(i):
                    n = (i - i0) * 8 + ((MIX_AT[0] if l == 0 else MIX_AT[3]) + (8 if first(i) else 12))
                    add_out(n, lambda d: (i - i0) * 6 + (outs + d))
                    wait("rg_so_full", i + 1)
                    if not (first(i) and i == 0):
                        wait("rg_stored", i * 64)
                    copy(rg_so[0:36], ps[0:36, 2:4, 320:448]).then_inc(S("rg_so_ready"), 1)

                def body(i, whole):
                    two = lambda v: v[:, :, bass.ds((i - i0) * 2, 2)]
                    did(copy(rg_cur[:, 0:4, :], two(par[:, 1, l * 64:(l + 1) * 64].rearrange("p (k t) -> p k t", k=4))))
                    did(copy(rg_cur[:, 4:9, :], two(rgc[:, :, l, :])))
                    wait("rg_ht_full", i + 1)
                    wait("rg_u_in", i + 1)
                    ht = ps[:, 1, 320:384].rearrange("p (t c) -> p t c", t=2)
                    did(copy(samples(rg_in, SC)[:, :, :, 0:3], ht[:, :, 0:24].rearrange("p t (b k) -> p t b k", b=NB)))
                    did(copy(rg_h0, ht[:, :, 24:32]))
                    sync()
                    for j in range(2):
                        did(ts(rg_u[:, j, 0:CV], rg_in[:, j, 0:CV], rg_cur[:, 0, j:j + 1], rg_cur[:, 4, j:j + 1], MUL, ADD))
                    for k in range(1, 4):
                        sync()
                        for j in range(2):
                            ins = stt(rg_u[:, j, 0:CV], rg_in[:, j, k:k + CV], rg_cur[:, k, j:j + 1], rg_u[:, j, 0:CV], MUL, ADD)
                            if k == 3 and j == 1:
                                ins.then_inc(S("rg_conv_done"), 1)
                            else:
                                did(ins)
                    wait("rg_gate_sig", i + 1)
                    tt(rg_gate, rg_gate, ps[:, 2:4, 0:NT], MUL).then_inc(S("rg_gate_read"), 1)
                    wait("rg_u_high", i + 1)
                    tt(ug[:, 1, :, 0:CV], rg_u[:, :, 0:CV], ug[:, 0, :, 0:CV].bitcast(F32), SUB).then_inc(S("rg_u_ready"), 1)
                    if whole:
                        finish(i - 1)
                    did(copy(rg_pack[:, :, 0:3], rg_in[:, :, SEQ:SEQ + 3]))
                    copy(rg_pack[:, :, 3:27].rearrange("p t (b k) -> p t b k", b=NB), samples(rg_in, SC)[:, :, :, NL:SEG]).then_inc(S("rg_in_read"), 1)
                    wait("rg_ri_read", i + 1)
                    did(tt(rg_i[:, :, 0:CV], rg_i[:, :, 0:CV], rg_u[:, :, 0:CV], MUL))
                    wait("rg_a_ready", i + 1)
                    stt(rg_t[:, :, 0:CV], rg_r[:, :, 0:CV], 1.0, rg_t[:, :, 0:CV], ADD, MUL).then_inc(S("rg_v_ready"), 1)
                    wait("rg_root", i + 1)
                    sync()
                    did(tt(rg_i[:, :, 0:CV], rg_i[:, :, 0:CV], rg_t[:, :, 0:CV], MUL))
                    first_a, first_b = samples(rg_a, SC)[:, :, :, 0], samples(rg_i, SC)[:, :, :, 0]
                    did(tt(rg_fix, first_a, rg_h0, MUL))
                    sync()
                    did(tt(first_b, first_b, rg_fix, ADD))
                    did(ts(first_a, first_a, 0.0, None, MUL))
                    sync()
                    for j in range(2):
                        did(dve.tensor_tensor_scan(rg_r[:, j, 0:CV], rg_a[:, j, 0:CV], rg_i[:, j, 0:CV], 0.0, MUL, ADD))
                    sync()
                    did(copy(rg_pack[:, :, 27:28], rg_r[:, :, SEQ - 1:SEQ]))
                    copy(rg_pack[:, :, 28:36], samples(rg_r, SC)[:, :, :, NL - 1]).then_inc(S("rg_pack_ready"), 1)
                    did(tt(rg_o[:, :, 0:SEQ], rg_r[:, :, 0:SEQ], rg_gate[:, :, 0:SEQ], MUL))
                    tt(by_seq(rg_o), apart(rg_r), by_seq(rg_gate), MUL).then_inc(S("rg_o_done"), 1)
                    wait("rg_o_high", i + 1)
                    tt(Ol[:, 0:2, :], rg_o, Oh[:, 0:2, :].bitcast(F32), SUB).then_inc(S("rg_o_ready"), 1)

                last = i0 + 7
                wait("h_ready", KD * (1 if l == 0 else 10))
                did(dve.memset(Y[:, :, :], 0.0))
                did(dve.memset(rg_in[:, :, 0:3], 0.0))
                for t in (rg_r, rg_a, rg_i):
                    did(dve.memset(t[:, :, CV:EXT], 0.0))
                body(i0, False)
                with dve.Fori(i0 + 1, i0 + GROUPS) as i:
                    steps.count.enter(i, i0 + 1, RG_DVE)
                    body(i, True)
                    steps.count.leave(GROUPS - 1)
                finish(last)

            def ssd():
                sm = slice(64, P)
                wait("h_ready", 4 * KD)
                did(dve.memset(Y[:, :, :], 0.0))
                did(dve.memset(sd_in[:, :, 0:3], 0.0))
                did(dve.memset(sd_c[:, :, CV:EXT], 0.0))
                did(dve.memset(sd_ta, 0.0))
                wait("sd_wdt_high", 1)
                tt(wdtl[:], wdt, wdth[:].bitcast(F32), SUB).then_inc(S("sd_wdt"), 1)
                wait("sd_dt_full", 1)
                wait("in_head", 64)
                three_ = lambda v: v.rearrange("p (t h) -> p t h", t=3)
                did(tt(three_(sd_tw[:, 0]), three_(ps[:, 0, 0:96]), dtb.unsqueeze(1).broadcast_to([P, 3, 32]), ADD))
                sync()
                stt(sd_tw[:, 1], sd_tw[:, 0], -1.0, sd_tw[:, 0], MUL, MAX).then_inc(S("sd_dt_abs"), 1)
                did(ts(sd_tw[:, 0], sd_tw[:, 0], 0.0, None, MAX))
                wait("sd_dt_exp", 1)
                log1p(sd_tw[:, 1], sd_tw[:, 2], sd_tw[:, 3], sd_tw[:, 4])
                did(tt(sd_ta[:, 0], three_(sd_tw[:, 0]), three_(sd_tw[:, 4]), ADD))
                wait("sd_a", 1)
                sync()
                stt(sd_ta[:, 1], sd_ta[:, 0], -1.0, alog.unsqueeze(1).broadcast_to([P, 3, 32]), MUL, MUL).then_inc(S("sd_dta"), 1)
                wait("sd_sums_read", 1)

                def last_rows(i):
                    wait("sd_so_full", i + 1)
                    if not (first(i) and i == 0):
                        wait("sd_so_out", i * 96)
                    copy(sd_so[0:27], ps[0:27, 4, :].rearrange("p (t c) -> p t c", t=4)).then_inc(S("sd_so_ready"), 1)

                def finish(i, last):
                    n = i * 8 + (MIX_AT[1] + (8 if last else 14))
                    add_out(n, lambda d: i * 6 + (6 * GROUPS + d))

                def history(i):
                    wait("sd_ht_full", i + 1)
                    wait("sd_in_ready", i + 1)
                    ht = ps[:, 1, 320:416].rearrange("p (t b k) -> p t b k", t=4, b=NB)
                    copy(samples(sd_in, SC)[:, :, :, 0:3], ht).then_inc(S("sd_ht_read"), 1)

                def enter(i, whole):
                    did(copy(sd_tc[:, 0:5], sd_ta[:, :, :, bass.ds(i * 4, 4)]))
                    taps = par[:, 3, :].rearrange("p (k g t) -> p k g t", k=4, g=4)
                    bias = par[:, 4, 0:32].rearrange("p (g t) -> p g t", g=4)
                    did(copy(sd_cur[:, 0:4, 0:2].unsqueeze(3), taps[:, :, 2:4, bass.ds(i, 1)]))
                    did(copy(sd_cur[:, 0:4, 2:4], par[:, 3, :].rearrange("p (k t) -> p k t", k=4)[:, :, bass.ds(i * 2, 2)]))
                    did(copy(sd_cur[:, 4, 0:2].unsqueeze(2), bias[:, 2:4, bass.ds(i, 1)]))
                    did(copy(sd_cur[:, 4, 2:4], par[:, 4, 0:16][:, bass.ds(i * 2, 2)]))
                    did(copy(sd_cur[:, 5, 0:2], dcol[:, bass.ds(i * 2, 2)]))
                    did(copy(sd_cur[:, 6, 0:2], par[:, 4, 32:48][:, bass.ds(i * 2, 2)]))
                    if first(i) and i == 0:
                        history(0)
                    wait("sd_in_ready", i + 1)
                    wait("sd_ht_read", i + 1)
                    sync()
                    for j in range(4):
                        did(ts(sd_c[:, j, 0:CV], sd_in[:, j, 0:CV], sd_cur[:, 0, j:j + 1], sd_cur[:, 4, j:j + 1], MUL, ADD))
                    for k in range(1, 4):
                        sync()
                        for j in range(4):
                            ins = stt(sd_c[:, j, 0:CV], sd_in[:, j, k:k + CV], sd_cur[:, k, j:j + 1], sd_c[:, j, 0:CV], MUL, ADD)
                            if k == 3 and j == 3:
                                ins.then_inc(S("sd_conv_done"), 1)
                            else:
                                did(ins)
                    did(copy(sd_pack[:, :, 0:3], sd_in[:, :, SEQ:SEQ + 3]))
                    copy(sd_pack[:, :, 3:27].rearrange("p t (b k) -> p t b k", b=NB), samples(sd_in, SC)[:, :, :, NL:SEG]).then_inc(S("sd_in_read"), 1)
                    wait("sd_z_sig", i + 1)
                    tt(sd_z, sd_z, ps[:, 0:2, 0:NT], MUL).then_inc(S("sd_z_read"), 1)
                    if whole:
                        finish(i - 1, False)
                    wait("sd_sig_ready", i + 1)
                    did(tt(sd_f[:, :, 0:SEQ], sd_sig[:, :, 0:SEQ], sd_c[:, :, 0:SEQ], MUL))
                    tt(by_seq(sd_f), by_seq(sd_sig), apart(sd_c), MUL).then_inc(S("sd_f_ready"), 1)

                def mix(i, last=False):
                    heads = lambda v, T: v.rearrange("p (t h c) -> p t h c", t=T, h=4)
                    wide = lambda v, n: v.unsqueeze(len(v.shape)).broadcast_to(list(v.shape) + [n])
                    wait("sd_xt_full", i + 1)
                    tt(sd_xt[:, 0:2], heads(ps[:, 4, :], 2), wide(sd_tc[:, 0, 0:2, :], 64), MUL).then_inc(S("sd_xt_read"), 1)
                    wait("sd_xs_full", i + 1)
                    did(tt(sd_xt[sm, 2:3], heads(ps[sm, 5, 0:256], 1), wide(sd_tc[sm, 0, 2:3, :], 64), MUL))
                    did(copy(sd_bt[sm, 2, :], ps[sm, 5, 256:384]))
                    tt(sd_bm[sm], ps[sm, 5, 256:384].unsqueeze(1).broadcast_to([64, NB, P]), wide(s_block[sm, :], P), MUL).then_inc(S("sd_xs_read"), 1)
                    wait("sd_cb_full", i + 1)
                    did(tt(sd_cb[:, 0:2], ps[:, 7, 0:256].rearrange("p (t c) -> p t c", t=2), upper[:].unsqueeze(1).broadcast_to([P, 2, P]), MUL))
                    tt(sd_cb[sm, 2, 0:64], ps[sm, 7, 256:320], s_causal[sm], MUL).then_inc(S("sd_cb_read"), 1)
                    for T, bank in ((0, 4), (1, 5)):
                        wait(f"sd_seg{T}_full", i + 1)
                        for h in range(4):
                            ins = ts(sd_e[:, T, h, :], ps[:, bank, h * P:(h + 1) * P], sd_tc[:, 2, T, h:h + 1], 0.0, SUB, MIN)
                            if h == 3:
                                ins.then_inc(S(f"sd_seg{T}_ready"), 1)
                            else:
                                did(ins)
                    wait("sd_seg2_full", i + 1)
                    for h in range(4):
                        ins = ts(sd_e[sm, 2, h, 0:64], ps[sm, 6, h * 64:(h + 1) * 64], sd_tc[sm, 2, 2, h:h + 1], 0.0, SUB, MIN)
                        if h == 3:
                            ins.then_inc(S("sd_seg2_ready"), 1)
                        else:
                            did(ins)
                    wait("sd_xt_read", i + 1)
                    sync()
                    did(tt(sd_xw[:, 0:2], sd_xt[:, 0:2], wide(sd_tc[:, 3, 0:2, :], 64), MUL))
                    did(tt(sd_xw[sm, 2:3], sd_xt[sm, 2:3], wide(sd_tc[sm, 3, 2:3, :], 64), MUL))
                    sync()
                    tt(sd_xf, sd_xw[:, 0], wide(sd_tc[:, 4, 0, :], 64), MUL).then_inc(S("sd_xw_ready"), 1)
                    wait("sd_cb_read", i + 1)
                    for T in range(2):
                        wait(f"sd_exp{T}", i + 1)
                        did(tt(sd_e[:, T], sd_e[:, T], sd_cb[:, T].unsqueeze(1).broadcast_to([P, 4, P]), MUL))
                    wait("sd_exp2", i + 1)
                    tt(sd_e[sm, 2, :, 0:64], sd_e[sm, 2, :, 0:64], sd_cb[sm, 2, 0:64].unsqueeze(1).broadcast_to([64, 4, 64]), MUL).then_inc(S("sd_m_ready"), 1)
                    wait("sd_eo_read", i + 1)
                    for t in range(2):
                        wait(f"sd_y{t}_full", i + 1)
                        did(tt(sd_yo[:, t, :], ps[:, 5 + t, 320:512], sd_eo[:, t, 0:192], MUL))
                        stt(sd_y[:, t, :], sd_f[:, 2 + t, :], sd_cur[:, 5, t:t + 1], ps[:, 5 + t, 0:NT], MUL, ADD).then_inc(S(f"sd_y{t}_read"), 1)
                        wait(f"sd_y{t}_read", i + 1)
                        sync()
                        did(tt(sd_y[:, t, P:NT], sd_y[:, t, P:NT], sd_yo[:, t, :], ADD))
                        sync()
                        tt(sd_y[:, t, :], sd_y[:, t, :], sd_z[:, t, :], MUL).then_inc(S("sd_yz_ready"), 1)
                    for n, bank in enumerate((7, 4, 5, 6)):
                        t, half = n // 2, n % 2
                        s0 = sd_s0[:, t, 4 * half:4 * half + 4, :]
                        did(tt(s0, s0, wide(sd_eo[:, t, 192 + 4 * half:196 + 4 * half], P), MUL))
                        wait(f"sd_sn{n}_full", i + 1)
                        sync()
                        tt(s0, s0, ps[:, bank, :].rearrange("p (b n) -> p b n", b=4), ADD).then_inc(S(f"sd_sn{n}_read"), 1)
                    if not last:
                        history(i + 1)
                    wait("sd_rs_ready", i + 1)
                    wait("sd_yz_ready", i * 2 + 2)
                    for t in range(2):
                        ins = stt(sd_y[:, t, :], sd_y[:, t, :], sd_cur[:, 6, t:t + 1], sd_rs, MUL, MUL)
                        if t == 0:
                            did(ins)
                        else:
                            ins.then_inc(S("sd_y_done"), 1)
                    wait("sd_o_high", i + 1)
                    tt(Ol[:, 0:2, :], sd_y, Oh[:, 0:2, :].bitcast(F32), SUB).then_inc(S("sd_o_ready"), 1)
                    last_rows(i)

                enter(0, False)
                mix(0)
                with dve.Fori(1, GROUPS - 1) as i:
                    steps.count.enter(i, 1, SSD_DVE)
                    enter(i, True)
                    mix(i)
                    steps.count.leave(GROUPS - 2)
                enter(7, True)
                mix(7, True)
                finish(7, True)

            def hg():
                sm = slice(64, P)
                wide = lambda v, n: v.unsqueeze(len(v.shape)).broadcast_to(list(v.shape) + [n])
                wait("h_ready", 7 * KD)
                did(dve.memset(hg_A[:, :, 0:1], 0.0))

                def head(i, h):
                    n = i * 2 + (h + 1)
                    wait("hg_kt_full", n)
                    copy(hg_kt, ps[:, 5, 0:384].rearrange("p (t c) -> p t c", t=3)).then_inc(S("hg_kt_read"), 1)
                    wait("hg_att_full", n)
                    did(tt(hg_att[h][:, 0:SEQ].rearrange("p (t c) -> p t c", t=2), ps[:, 4, 0:SEQ].rearrange("p (t c) -> p t c", t=2),
                           upper[:].unsqueeze(1).broadcast_to([P, 2, P]), MUL))
                    tt(hg_att[h][sm, SEQ:NT], ps[sm, 4, SEQ:NT], s_causal[sm], MUL).then_inc(S("hg_att_ready"), 1)
                    wait("hg_s1_read", n)
                    wait("hg_s2_full", n)
                    if h == 0 and not (first(i) and i == 0):
                        wait("hg_stored", i * 48)
                    stt(hg_sf[:, h, :], hg_s1[:, h, :], hg_eA[:, 2 * h + 1, 8:9], ps[:, 4, 384:512], MUL, ADD).then_inc(S("hg_sf_read"), 1)
                    wait("hg_o_full", n)
                    wait("hg_osq_ready", n)
                    tt(hg_o[:, h, :], ps[:, 6, 0:NT], hg_g[:, h, :], MUL).then_inc(S("hg_o_read"), 1)
                    for half in range(2):
                        s0 = hg_s0[:, h, 4 * half:4 * half + 4, :]
                        did(tt(s0, s0, wide(hg_eg[:, h, 4 * half:4 * half + 4], P), MUL))
                        wait("hg_sn_full", i * 4 + (2 * h + half + 1))
                        sync()
                        tt(s0, s0, ps[:, 7, :].rearrange("p (b n) -> p b n", b=4), ADD).then_inc(S("hg_sn_read"), 1)

                def finish(i):
                    did(copy(hg_cur[:, 2, :], par[:, 4, 48:64][:, bass.ds(i * 2, 2)]))
                    wait("hg_rs_ready", i + 1)
                    wait("hg_o_read", i * 2 + 2)
                    sync()
                    for h in range(2):
                        did(stt(hg_o[:, h, :], hg_o[:, h, :], hg_cur[:, 2, h:h + 1], hg_rs[:, h, :], MUL, MUL))
                    sync()
                    did(copy(Oh16[:, bass.ds(i * 2, 2), :], hg_o))
                    sync()
                    tt(Ol16[:, bass.ds(i * 2, 2), :], hg_o, Oh16[:, bass.ds(i * 2, 2), :].bitcast(F32), SUB).then_inc(S("hg_o_ready"), 1)

                def body(i, mixed):
                    if mixed:
                        head(i - 1, 0)
                        head(i - 1, 1)
                    did(copy(hg_cur[:, 0, :], lb[:, bass.ds(i * 2, 2)]))
                    did(copy(hg_cur[:, 1, :], oml[:, bass.ds(i * 2, 2)]))
                    wait("hg_g_sig", i + 1)
                    tt(hg_g, hg_g, ps[:, 0:2, 0:NT], MUL).then_inc(S("hg_g_read"), 1)
                    wait("hg_q_sig", i + 1)
                    tt(hg_q, hg_q, ps[:, 2:4, 0:NT], MUL).then_inc(S("hg_q_read"), 1)
                    wait("hg_f_read", i + 1)
                    sync()
                    did(ts(hg_f[:, 0, :], hg_f[:, 0, :], hg_cur[:, 1, 0:1], hg_cur[:, 0, 0:1], MUL, ADD))
                    ts(hg_f[:, 1, :], hg_f[:, 1, :], hg_cur[:, 1, 1:2], hg_cur[:, 0, 1:2], MUL, ADD).then_inc(S("hg_forget"), 1)
                    if mixed:
                        finish(i - 1)
                    wait("hg_logf", i + 1)
                    for h in range(2):
                        did(dve.tensor_tensor_scan(hg_G[:, h, :], restart[:], hg_f[:, h, :], 0.0, MUL, ADD))
                    sync()
                    ends = hg_G[:, :, 0:SEQ].rearrange("p h (c s) -> p h c s", s=16)
                    ends_s = by_seq(hg_G)
                    did(copy(hg_gt[:, :, 0:16], ends[:, :, :, 15]))
                    did(copy(hg_gt[:, :, 16:24], ends_s[:, :, :, 7]))
                    did(tt(hg_x[:, :, 0:SEQ].rearrange("p h (c s) -> p h c s", s=16), ends[:, :, :, 15:16].broadcast_to([P, 2, 16, 16]), ends, SUB))
                    did(tt(by_seq(hg_x), ends_s[:, :, :, 7:8].broadcast_to([P, 2, NB, NL]), ends_s, SUB))
                    sync()
                    for h in range(2):
                        did(dve.tensor_tensor_scan(hg_gt[:, h, 24:40], r16, hg_gt[:, h, 0:16], 0.0, MUL, ADD))
                    sync()
                    B = hg_gt[:, :, 24:40].rearrange("p h (t c) -> p h t c", t=2)
                    Bd = hg_B
                    did(copy(Bd[:].rearrange("p (h t) c -> p h t c", h=2), B))
                    did(copy(hg_A[:, :, 1:9].rearrange("p (h t) c -> p h t c", h=2), B))
                    sync()
                    Dv = hg_D.rearrange("p r (a b) -> p r a b", b=8)
                    did(tt(Dv, wide(hg_A[:], 8), Bd[:].unsqueeze(2).broadcast_to([P, 4, 9, 8]), SUB))
                    sync()
                    tt(hg_D, hg_D, dmask[:].unsqueeze(1).broadcast_to([P, 4, 72]), MUL).then_inc(S("hg_G_ready"), 1)
                    wait("hg_q_read", i + 1)
                    wait("hg_exps", i + 1)
                    did(tt(hg_q, hg_q, hg_G, MUL))
                    for h in range(2):
                        did(stt(hg_k[:, h, :], hg_k[:, h, :], hg_cur[:, 1, h:h + 1], hg_x[:, h, :], MUL, MUL))
                    sync()
                    for h in range(2):
                        for T in range(2):
                            kd = hg_k[:, h, T * P:(T + 1) * P].rearrange("p (c s) -> p c s", s=16)
                            did(tt(hg_K[2 * h + T].rearrange("p a (c s) -> p a c s", s=16), kd.unsqueeze(1).broadcast_to([P, 9, 8, 16]),
                                   wide(hg_D[:, 2 * h + T, :].rearrange("p (a b) -> p a b", b=8), 16), MUL))
                    did(tt(hg_ks.rearrange("p h (b s) -> p h b s", b=NB), by_seq(hg_k), wide(hg_en[:], NL), MUL))
                    for h in range(2):
                        ins = tt(hg_x[:, h, 0:P].rearrange("p (c s) -> p c s", s=16), hg_q[:, h, P:2 * P].rearrange("p (c s) -> p c s", s=16),
                                 wide(hg_eA[:, 2 * h + 1, 0:8], 16), MUL)
                        if h == 0:
                            did(ins)
                        else:
                            ins.then_inc(S("hg_K_ready"), 1)
                    wait("hg_v_read", i + 1)
                    tt(hg_vm[sm], hg_v[sm, 2, :].unsqueeze(1).broadcast_to([64, NB, 256]), wide(s_block[sm, :], 256), MUL).then_inc(S("hg_vm_ready"), 1)

                r16 = restart[:, SEQ:SEQ + 16]
                body(0, False)
                with dve.Fori(1, GROUPS) as i:
                    steps.count.enter(i, 1, HG_DVE)
                    body(i, True)
                    steps.count.leave(GROUPS - 1)
                head(7, 0)
                head(7, 1)
                finish(7)
                wait("hg_stored", GROUPS * 48)
                for t in range(KD):
                    dve.wait_ge(used, OUT_AT + 4 * (t // 2) + 3 + t % 2)
                    copy(Y[:, t], ps[:, t % 4, 0:NT]).then_inc(S("y_added"), 1)

            def attention(L):
                name, n = (("rg_stored", 8 * 64), ("sd_stored", 8 * 48), ("hg_stored", 8 * 48), ("rg_stored", 16 * 64))[L]
                wait(name, n)
                if L == 1:
                    wait("sd_so_out", 8 * 96)
                g = lambda k: par[:, 5, L * 8 + k:L * 8 + k + 1]
                normal(3 * L + 1, None, memn, g, memh, NMEM)
                residual(2 + 4 * L, gain(L, 1))
                for h in range(2 * XH):
                    wait("at_turned_full", 2 * XH * L + h + 1)
                    turned = ps[:, 4 + h % 2, :].rearrange("p (a d) -> p a d", a=2)
                    if h < XH:
                        if h >= 2:
                            wait(f"at_k_out{h % 2}", 16 * (2 * L + 1))
                        copy(at_k[:, h % 2], turned).then_inc(S("at_k_ready"), 1)
                    else:
                        copy(at_v[:, :, (h - XH) * 256:(h - XH + 1) * 256], turned).then_inc(S("at_v_ready"), 1)
                normal(3 * L + 2, 3 + 4 * L, X, gain(L, 2))
                wait("h_ready", KD * (3 * L + 3))
                dve.sem_inc(S("at_area"), 1)
                did(dve.memset(work[:, 2048:4096], 0.0))
                for t in range(KD):
                    dve.wait_ge(used, ATT_AT[L] + 16 + t + 1)
                    ts(at_q[:, t], ps[:, t % 4, 0:NT], 256.0 ** -0.5, None, MUL).then_inc(S("at_q_ready"), 1)
                wait("at_q_ready", KD * (L + 1))
                sync()
                for h in range(XH):
                    ins = copy(at_qz[:, :, 2 * h:2 * h + 2, NL * h:NL * (h + 1)],
                               at_q[:, 2 * h:2 * h + 2, SEQ:NT].rearrange("p c (b l) -> p b c l", b=NB))
                    if h < XH - 1:
                        did(ins)
                    else:
                        ins.then_inc(S("at_qz_ready"), 1)
                for n in range(16):
                    wait("at_kb_used", 32 * L + n + 1)
                    if n >= 2:
                        wait("at_cs_full", 16 * L + n - 1)
                    copy(at_kbt[:, n % 2, 4:8, :], ps[:, 5, :].rearrange("p (c m) -> p c m", c=4)).then_inc(S("at_kbt1_ready"), 1)
                two = lambda v: v.rearrange("p b (h m) -> p b h m", h=2)
                for T in range(2):
                    wait("at_s_full", 2 * L + T + 1)
                    did(dve.tensor_reduce(at_m[:, 1 + T, 0:4].rearrange("p (b h) -> p b h", b=2), two(ps[:, 2 * T:2 * T + 2, :]), axis=AX, op=MAX))
                    sync()
                    ts(at_m[:, 1 + T, 0:4], at_m[:, 1 + T, 0:4], -1.0, None, MUL).then_inc(S("at_m_ready"), 1)
                wait("at_cs_full", 16 * L + 16)
                did(dve.memset(at_kt, 0.0))
                did(dve.tensor_reduce(at_m[:, 5, 0:2], ps[:, 7, :].rearrange("p (b m) -> p b m", b=2), axis=AX, op=MAX))
                sync()
                ts(at_m[:, 5, 0:2], at_m[:, 5, 0:2], -1.0, None, MUL).then_inc(S("at_ms_ready"), 1)
                for T in range(2):
                    wait("at_e_ready", 2 * L + T + 1)
                    did(dve.reciprocal(at_m[:, 3 + T, 0:4], at_m[:, 3 + T, 0:4]))
                    sync()
                    for h in range(XH):
                        ins = ts(at_pp[:, h, :], at_pp[:, h, :], at_m[:, 3 + T, h:h + 1], None, MUL)
                        if h < XH - 1:
                            did(ins)
                        else:
                            ins.then_inc(S("at_pp_ready"), 1)
                    for k in range(2):
                        wait("at_ppt_full", 4 * L + 2 * T + k + 1)
                        copy(at_ppt[:, 2 * k:2 * k + 2, :, T * P:(T + 1) * P], ps[:, 4 + k, :].rearrange("p (h a m) -> p h a m", h=2, a=2)).then_inc(S("at_ppt_read"), 1)
                wait("at_es_ready", L + 1)
                did(dve.reciprocal(at_m[:, 6, 0:2], at_m[:, 6, 0:2]))
                sync()
                did(ts(at_p[:, 0, :], at_p[:, 0, :], at_m[:, 6, 0:1], None, MUL))
                ts(at_p[:, 1, :], at_p[:, 1, :], at_m[:, 6, 1:2], None, MUL).then_inc(S("at_p_ready"), 1)
                wait("at_pt_full", L + 1)
                pt = ps[:, 6, :].rearrange("p (a b h l) -> p a b h l", a=2, b=NB, h=XH)
                for h in range(XH):
                    ins = copy(at_ptz[:, :, :, h, NL * h:NL * (h + 1)], pt[:, :, :, h, :])
                    if h < XH - 1:
                        did(ins)
                    else:
                        ins.then_inc(S("at_pt_ready"), 1)
                wait("at_o_full", L + 1)
                did(copy(at_q[:, :, 0:SEQ].rearrange("p (b c) m -> p b c m", c=2), two(ps[:, 0:4, :])))
                wait("at_so_full", L + 1)
                for hb in range(2):
                    for c in range(2):
                        c0 = SEQ + 32 * hb
                        out = at_q.rearrange("p (h c) n -> p h c n", c=2)[:, :, c, c0:c0 + 32].rearrange("p h (b l) -> p b h l", l=NL)
                        ins = copy(out, ps[:, 6, 256 * hb + P * c:256 * hb + P * (c + 1)].rearrange("p (b h l) -> p b h l", b=4, h=XH))
                        if hb == 0 or c == 0:
                            did(ins)
                        else:
                            ins.then_inc(S("at_o_whole"), 1)
                wait("at_o_high", L + 1)
                tt(Ol[:], at_q, Oh[:].bitcast(F32), SUB).then_inc(S("at_o_ready"), 1)
                residual(4 + 4 * L, gain(L, 3))
                wait("at_k_out0", (L + 1) * 32)
                wait("at_k_out1", (L + 1) * 32)
                wait("at_v_out", (L + 1) * 16)
                if L < DEPTH - 1:
                    normal(3 * L + 3, 5 + 4 * L, X, gain(L + 1, 0))

            rg(0)
            attention(0)
            ssd()
            attention(1)
            hg()
            attention(2)
            rg(1)
            attention(3)
            for k in range(KD):
                wait("yt_full", k + 1)
                did(copy(x_rows[:, 0:2, k * P:(k + 1) * P], ps[:, k, 0:SEQ].rearrange("p (a c) -> p a c", a=2)))
                ins = copy(x_rows[64:P, 2, k * P:(k + 1) * P], ps[64:P, k, SEQ:SEQ + P])
                if k < KD - 1:
                    did(ins)
                else:
                    ins.then_inc(S("y_ready"), 1)


INPUTS = {
    "x_prompt": (1, SEQ, D), "x_sample": (NB, NL, D), "mem_prompt": (1, NMEM, D),
    "state_rglru_conv": (2, NB, 3, BR), "state_rglru_h": (2, NB, BR), "state_ssd_conv": (1, NB, 3, 2 * BR),
    "state_ssd": (1, NB, 32, 64, P), "state_hgrn": (1, NB, 16, P, P),
    "cache_mem_k": (DEPTH, NB, NMEM, XH, 256), "cache_mem_v": (DEPTH, NB, NMEM, XH, 256),
    "norm_g": (DEPTH, 4, D), "mem_norm_g": (DEPTH, D), "rg_w_in": (2, D, 2 * BR), "rg_conv_w": (2, 4, BR),
    "rg_conv_b": (2, BR), "rg_w_a": (2, 8, 256, 256), "rg_b_a": (2, BR), "rg_w_x": (2, 8, 256, 256),
    "rg_b_x": (2, BR), "rg_lambda": (2, BR), "rg_w_out": (2, BR, D), "ssd_w_in": (1, D, 3 * BR + 32),
    "ssd_conv_w": (1, 4, 2 * BR), "ssd_conv_b": (1, 2 * BR), "ssd_dt_bias": (1, 32), "ssd_a_log": (1, 32),
    "ssd_d": (1, 32), "ssd_norm_g": (1, BR), "ssd_w_out": (1, BR, D), "hg_w_in": (1, D, 4 * BR),
    "hg_lower_bounds": (DEPTH, BR), "hg_norm_g": (1, BR), "hg_w_out": (1, BR, D),
    "x_w_q": (DEPTH, D, D), "x_w_k": (DEPTH, D, D), "x_w_v": (DEPTH, D, D), "x_w_o": (DEPTH, D, D),
}
OUTPUTS = {
    "y_p": (1, SEQ, D), "y_s": (NB, NL, D), "rgc_p": (2, 1, 3, BR), "rgh_p": (2, 1, BR), "sc_p": (1, 1, 3, 2 * BR),
    "ss_p": (1, 1, 32, 64, P), "hs_p": (1, 1, 16, P, P), "mk": (DEPTH, 1, NMEM, XH, 256),
    "mv": (DEPTH, 1, NMEM, XH, 256), "rgc_s": (2, NB, 3, BR), "rgh_s": (2, NB, BR), "sc_s": (1, NB, 3, 2 * BR),
    "ss_s": (1, NB, 32, 64, P), "hs_s": (1, NB, 16, P, P),
}


def kernel(**inputs):
    import numpy as np
    import concourse.bacc as _bacc
    from concourse.bass_utils import run_bass_kernel_spmd as _run

    nc = _bacc.Bacc("TRN2", target_bir_lowering=False, num_devices=1)
    arrays = {n: np.ascontiguousarray(inputs[n]) for n in INPUTS}
    ins = {n: nc.dram_tensor(n, s, F32, kind="ExternalInput").ap() for n, s in INPUTS.items()}
    outs = {n: nc.dram_tensor("out_" + n, s, F32, kind="ExternalOutput").ap() for n, s in OUTPUTS.items()}
    trunk(nc, ins, outs)
    result = _run(nc, [arrays], core_ids=[0]).results[0]
    return tuple(result["out_" + n] for n in OUTPUTS)
```
